# Optimizing a Trainium2 kernel written in Bass

```python
import jax, jax.numpy as jnp
from jax import lax
import numpy as np

D_MODEL = 2048
BATCH = 1
SEQ = 256
DEPTH = 1

CHUNK = 64
Q_BLOCK = 128
CONV_WIDTH = D_MODEL // 2
CONV_GROUPS = 8
CONV_K = 3
V_DIM = 128
N_HEADS = (D_MODEL - CONV_WIDTH) // V_DIM
QK_NOPE = 128
QK_ROPE = 64
Q_RANK = 768
KV_RANK = 512
ATTN_WIDTH = N_HEADS * V_DIM
MIX_WIDTH = CONV_WIDTH + ATTN_WIDTH
IN_WIDTH = 3 * CONV_WIDTH + Q_RANK + KV_RANK + QK_ROPE
D_FF = 4 * D_MODEL
ROPE_THETA = 10000.0
EPS = 1e-6
NEG_INF = -1e30

kernel_name = "hybrid_conv_mla_sandwich_block"

def rms_norm(x, g):
    x32 = x.astype(jnp.float32)
    y = x32 * lax.rsqrt(jnp.mean(x32 * x32, axis=-1, keepdims=True) + EPS)
    return (y * g.astype(jnp.float32)).astype(x.dtype)

def group_rms_norm(x, g, n_groups):
    b, s, w = x.shape
    y = rms_norm(x.reshape(b, s, n_groups, w // n_groups), g.reshape(n_groups, w // n_groups))
    return y.reshape(b, s, w)

def apply_rope(x, cos, sin):
    x32 = x.astype(jnp.float32)
    x1, x2 = jnp.split(x32, 2, axis=-1)
    return jnp.concatenate([x1 * cos - x2 * sin, x2 * cos + x1 * sin], axis=-1).astype(x.dtype)

def short_conv_causal(u, w):
    rhs = w[:, None, :].astype(u.dtype)
    return lax.conv_general_dilated(
        u, rhs, window_strides=(1,), padding=[(CONV_K - 1, 0)],
        dimension_numbers=("NWC", "WIO", "NWC"), feature_group_count=u.shape[-1])

def chunk_causal_mla(q_nope, q_rope, k_nope, k_rope, v):
    s_len = q_nope.shape[1]
    scale = (QK_NOPE + QK_ROPE) ** -0.5
    chunk_id = jnp.arange(s_len) // CHUNK
    outs = []
    for start in range(0, s_len, Q_BLOCK):
        end = start + Q_BLOCK
        s = (jnp.einsum("bqhd,bkhd->bhqk", q_nope[:, start:end], k_nope[:, :end],
                        preferred_element_type=jnp.float32)
             + jnp.einsum("bqhr,bkr->bhqk", q_rope[:, start:end], k_rope[:, :end],
                          preferred_element_type=jnp.float32)) * scale
        visible = chunk_id[None, :end] <= chunk_id[start:end, None]
        s = jnp.where(visible, s, NEG_INF)
        p = jax.nn.softmax(s, axis=-1).astype(v.dtype)
        outs.append(jnp.einsum("bhqk,bkhd->bqhd", p, v[:, :end]))
    return jnp.concatenate(outs, axis=1)

def hybrid_mixer(h, w_in, conv_w, q_norm_g, w_uq, kv_norm_g, w_ukv, conv_out_g, attn_out_g, w_o):
    b, s, _ = h.shape
    proj = h @ w_in
    cuts = np.cumsum([CONV_WIDTH, CONV_WIDTH, CONV_WIDTH, Q_RANK, KV_RANK]).tolist()
    u, gate_b, gate_c, c_q, c_kv, k_rope_raw = jnp.split(proj, cuts, axis=-1)

    y_conv = gate_b * short_conv_causal(gate_c * u, conv_w)
    y_conv = group_rms_norm(y_conv, conv_out_g, CONV_GROUPS)

    q = (rms_norm(c_q, q_norm_g) @ w_uq).reshape(b, s, N_HEADS, QK_NOPE + QK_ROPE)
    q_nope, q_rope = q[..., :QK_NOPE], q[..., QK_NOPE:]
    kv = (rms_norm(c_kv, kv_norm_g) @ w_ukv).reshape(b, s, N_HEADS, QK_NOPE + V_DIM)
    k_nope, v = kv[..., :QK_NOPE], kv[..., QK_NOPE:]
    pos = jnp.arange(s, dtype=jnp.float32)
    inv_freq = jnp.power(ROPE_THETA, -jnp.arange(0, QK_ROPE, 2, dtype=jnp.float32) / QK_ROPE)
    ang = pos[:, None] * inv_freq[None, :]
    cos, sin = jnp.cos(ang), jnp.sin(ang)
    q_rope = apply_rope(q_rope, cos[None, :, None, :], sin[None, :, None, :])
    k_rope = apply_rope(k_rope_raw, cos[None], sin[None])
    o = chunk_causal_mla(q_nope, q_rope, k_nope, k_rope, v)
    y_attn = group_rms_norm(o.reshape(b, s, ATTN_WIDTH), attn_out_g, N_HEADS)

    return jnp.concatenate([y_conv, y_attn], axis=-1) @ w_o

def setup_inputs(seed: int = 0) -> dict:
    key = jax.random.key(seed)
    ks = jax.random.split(key, 17)

    def w(k, shape, fan_in):
        return jax.random.normal(k, shape, jnp.float32) * (fan_in ** -0.5)

    def gain(k, n):
        return 1.0 + 0.05 * jax.random.normal(k, (DEPTH, n), jnp.float32)

    return {
        "x": jax.random.normal(ks[0], (BATCH, SEQ, D_MODEL), jnp.float32),
        "pre_mix_g": gain(ks[1], D_MODEL),
        "w_in": w(ks[2], (DEPTH, D_MODEL, IN_WIDTH), D_MODEL),
        "conv_w": w(ks[3], (DEPTH, CONV_K, CONV_WIDTH), CONV_K),
        "q_norm_g": gain(ks[4], Q_RANK),
        "w_uq": w(ks[5], (DEPTH, Q_RANK, N_HEADS * (QK_NOPE + QK_ROPE)), Q_RANK),
        "kv_norm_g": gain(ks[6], KV_RANK),
        "w_ukv": w(ks[7], (DEPTH, KV_RANK, N_HEADS * (QK_NOPE + V_DIM)), KV_RANK),
        "conv_out_g": gain(ks[8], CONV_WIDTH),
        "attn_out_g": gain(ks[9], ATTN_WIDTH),
        "w_o": w(ks[10], (DEPTH, MIX_WIDTH, D_MODEL), MIX_WIDTH),
        "post_mix_g": gain(ks[11], D_MODEL),
        "pre_mlp_g": gain(ks[12], D_MODEL),
        "w_up": w(ks[13], (DEPTH, D_MODEL, D_FF), D_MODEL),
        "w_down": w(ks[14], (DEPTH, D_FF, D_MODEL), D_FF),
        "post_mlp_g": gain(ks[15], D_MODEL),
    }

def reference(x, pre_mix_g, w_in, conv_w, q_norm_g, w_uq, kv_norm_g, w_ukv, conv_out_g,
              attn_out_g, w_o, post_mix_g, pre_mlp_g, w_up, w_down, post_mlp_g):
    for l in range(DEPTH):
        h = rms_norm(x, pre_mix_g[l])
        y = hybrid_mixer(h, w_in[l], conv_w[l], q_norm_g[l], w_uq[l], kv_norm_g[l], w_ukv[l],
                         conv_out_g[l], attn_out_g[l], w_o[l])
        x = x + rms_norm(y, post_mix_g[l])
        h = rms_norm(x, pre_mlp_g[l])
        m = jnp.square(jax.nn.relu(h @ w_up[l])) @ w_down[l]
        x = x + rms_norm(m, post_mlp_g[l])
    return x


_drawn_inputs = setup_inputs


def setup_inputs(seed=0):
    import zlib

    import numpy as np

    out = dict(_drawn_inputs(seed))
    spreads = {}
    factors = {}
    for name, (base, spread) in spreads.items():
        noise = np.random.default_rng([zlib.crc32(name.encode()), seed]).standard_normal(out[name].shape)
        drawn = base * np.exp(spread * noise) if base else spread * noise
        out[name] = __import__('jax').numpy.asarray(drawn.astype(out[name].dtype))
    for name, factor in factors.items():
        out[name] = (out[name] * factor).astype(out[name].dtype)
    return out
```

```python
from contextlib import ExitStack

import concourse.bass as bass
from concourse import mybir

F32 = mybir.dt.float32
F32R = mybir.dt.float32r
ALU = mybir.AluOpType
ACT = mybir.ActivationFunctionType
AX_X = mybir.AxisListType.X

P = 128
SEQ = 256
TB = SEQ // P
D = 2048
CW = 1024
N_HEADS = 8
NOPE = 128
ROPE = 64
V_DIM = 128
Q_RANK = 768
KV_RANK = 512
D_FF = 8192
CHUNK = 64
EPS = 1e-6
SCALE = float(NOPE + ROPE) ** -0.5
MASKED = -1e30

W = 512
KC = D // P
LAT = Q_RANK + KV_RANK + ROPE
LAT0 = 3 * CW
PAIRS = N_HEADS // 2
QW = 2 * (NOPE + ROPE)
FF_STRIPS = D_FF // W
RAW = 4
AHEAD = 4

G_MIX, G_MLP, G_Q, G_KV, G_CONV, G_ATT, G_TAP = 0, 16, 32, 38, 42, 50, 58
G_ROWS = G_TAP + 3 * (CW // P)

S_LAT, S_CONV, S_OUT = 0, 3, 9
CONV_PARTS = "ucb" * 2


def plan():
    steps, quads = [], []

    def quad(kind, **kw):
        n = len(quads)
        quads.append(dict(kind=kind, **kw))
        return n

    def mm(n, k):
        steps.append(("mm", n, k))

    for s in range(3):
        width = min(W, LAT - s * W)
        for q in range(4):
            if s == 0:
                steps.append(("xT", 2 * q, 0))
                steps.append(("xT", 2 * q + 1, 0))
            n = quad("in", strip=s, q=q, nk=4, width=width, col=LAT0 + s * W, first=q == 0, last=q == 3)
            for k in range(4):
                mm(n, k)
        if s == 0:
            steps.append(("x_stats", 0, 0))
        steps.append(("lat_out", s, n))
    steps.append(("lat_norm", 0, 0))

    def between(sub):
        if sub == 6:
            steps.extend([("latT", 0, 0), ("latT", 1, 0), ("krT", 0, 0), ("latT", 2, 0)])
        if sub == 9:
            steps.extend([("latT", 3, 0), ("latT", 4, 0)])
        for p in range(PAIRS):
            at = sub - 16 - 16 * p
            if at == 0:
                n = quad("kv", p=p, nk=4, width=W)
                for k in range(4):
                    mm(n, k)
                steps.append(("kv_out", p, n))
            if at == 4:
                for part in range(2):
                    n = quad("q", p=p, part=part, nk=3, width=QW)
                    for k in range(3):
                        mm(n, k)
                steps.append(("q_out", p, n))
            for when, what, h in [(5, "kT", 0), (6, "qT", 0), (9, "qrT", 0), (11, "scores", 0),
                                  (12, "scores", 1), (14, "probsT", 0), (15, "probsT", 1), (18, "pv", 0),
                                  (20, "o_squares", 0), (21, "o_norm", 0), (23, "oT", 0)]:
                if at == when:
                    steps.append((what, p, h))
        for c in range(4):
            for half, t, s, q in [(0, [49, 54, 59, 63][c], [51, 56, 61, 65][c], [52, 57, 62, 66][c]),
                                  (1, 97 + 3 * c, 99 + 3 * c, 101 + 3 * c)]:
                if sub == t:
                    steps.append(("convT", half, c))
                if sub == s:
                    steps.append(("conv_square", half, c))
                if sub == q:
                    steps.append(("conv_norm", half, c))

    sub = 0
    for i, part in enumerate(CONV_PARTS):
        col = CW * "ubc".index(part) + W * (i // 3)
        for q in range(4):
            between(sub)
            n = quad("in", strip=S_CONV + i, q=q, nk=4, width=W, col=col, first=q == 0, last=q == 3)
            for k in range(4):
                if k:
                    between(sub)
                mm(n, k)
                sub += 1
        steps.append(("conv_out", i, n))

    order = [(0, 2), (0, 3), (0, 0), (1, 2), (1, 3), (1, 0), (0, 1), (1, 1)]
    order += [(s, q) for s in (2, 3) for q in (2, 3, 0, 1)]
    for s, q in order:
        between(sub)
        n = quad("out", strip=S_OUT + s, q=q, nk=4, width=W, col=s * W, first=q == 2, last=q == 1)
        for k in range(4):
            if k:
                between(sub)
            mm(n, k)
            sub += 1
        if q == 1:
            steps.append(("y_out", s, n))
    steps.append(("y_norm", 0, 0))
    for q in range(4):
        steps.append(("x2", q, 0))
        steps.append(("hT", 2 * q, 0))
        steps.append(("hT", 2 * q + 1, 0))
        n = quad("up0", q=q, nk=4, width=W, first=q == 0, last=q == 3)
        if q < 3:
            for k in range(4):
                mm(n, k)
    steps.append(("x2_stats", 0, 0))
    for k in range(4):
        mm(n, k)
    steps.append(("relu", 0, 0))
    steps.append(("aT", 0, 0))
    return steps, quads


def hybrid_block(nc, t, out):
    steps, quads = plan()
    NQ = len(quads)
    assert NQ % RAW == 0 and (2 * NQ) % AHEAD == 0
    NQ_ALL = NQ + 8 * (FF_STRIPS - 1) + 4

    with ExitStack() as ctx:
        def sem(name):
            return ctx.enter_context(nc.semaphore(name))

        def tensor(stack, name, shape, dt=F32):
            return stack.enter_context(nc.sbuf_tensor(name, shape, dt))

        ident = tensor(ctx, "ident", [P, P])
        ones = tensor(ctx, "ones", [P, P])
        gain_rows = tensor(ctx, "gain_rows", [P, P])
        gains = tensor(ctx, "gains", [P, G_ROWS])
        neg_half = tensor(ctx, "neg_half", [P, 4])
        ss_x = tensor(ctx, "ss_x", [P, TB])
        rstd_x = tensor(ctx, "rstd_x", [P, TB])
        rstd_x2 = tensor(ctx, "rstd_x2", [P, TB])
        ss_lat = tensor(ctx, "ss_lat", [P, 4])
        rstd_lat = tensor(ctx, "rstd_lat", [P, 4])
        row_max = tensor(ctx, "row_max", [P, 4])
        neg_max = tensor(ctx, "neg_max", [P, 4])
        row_sum = tensor(ctx, "row_sum", [P, 4])
        inv_sum = tensor(ctx, "inv_sum", [P, 4])
        ss_o = tensor(ctx, "ss_o", [P, 4])
        rstd_o = tensor(ctx, "rstd_o", [P, 4])
        ss_strip = tensor(ctx, "ss_strip", [P, TB, 4])
        ss_row = tensor(ctx, "ss_row", [P, TB])
        rstd_row = tensor(ctx, "rstd_row", [P, TB])
        mean_sq = tensor(ctx, "mean_sq", [P, 6, 4])
        eps_col = tensor(ctx, "eps_col", [P, 1])
        xT_hi = tensor(ctx, "xT_hi", [P, KC, SEQ], F32R)
        xT_lo = tensor(ctx, "xT_lo", [P, KC, SEQ], F32R)
        yT_hi = tensor(ctx, "yT_hi", [P, KC, SEQ], F32R)
        yT_lo = tensor(ctx, "yT_lo", [P, KC, SEQ], F32R)
        raw = tensor(ctx, "raw", [P, RAW, 4 * W])
        w_hi = tensor(ctx, "w_hi", [P, AHEAD, 2 * W], F32R)
        w_lo = tensor(ctx, "w_lo", [P, AHEAD, 2 * W], F32R)
        KV_AT = 4
        with ExitStack() as mixer:
            cqT_hi = tensor(mixer, "cqT_hi", [P, Q_RANK // P, SEQ], F32R)
            cqT_lo = tensor(mixer, "cqT_lo", [P, Q_RANK // P, SEQ], F32R)
            lat = tensor(mixer, "lat", [P, TB, LAT])
            krT = tensor(mixer, "krT", [P, SEQ])
            kr_rot = tensor(mixer, "kr_rot", [P, TB, 2, ROPE])
            cos_t = tensor(mixer, "cos_t", [P, TB, 2 * ROPE])
            sin_t = tensor(mixer, "sin_t", [P, TB, 2 * ROPE])
            rope_c = tensor(mixer, "rope_c", [P, 2, ROPE])
            rope_s = tensor(mixer, "rope_s", [P, 2, ROPE])
            with ExitStack() as early:
                x_in = tensor(early, "x_in", [P, TB, D])
            u_sb = tensor(mixer, "u_sb", [P, TB, W])
            b_sb = tensor(mixer, "b_sb", [P, TB, W])
            q_sb = tensor(mixer, "q_sb", [P, TB, QW])
            qr_rot = tensor(mixer, "qr_rot", [P, TB, 2, ROPE])
            k_sb = tensor(mixer, "k_sb", [P, TB, 2, NOPE])
            v_sb = tensor(mixer, "v_sb", [P, 2, TB, 2, V_DIM])
            kT_sb = tensor(mixer, "kT_sb", [P, 2, SEQ])
            qT_sb = tensor(mixer, "qT_sb", [P, 2, SEQ])
            qrT_sb = tensor(mixer, "qrT_sb", [P, SEQ])
            probs = tensor(mixer, "probs", [P, 2, 3 * P])
            probsT = tensor(mixer, "probsT_sb", [P, 2, 3 * P])
            o_sb = tensor(mixer, "o_sb", [P, 2, TB, V_DIM])
            o_sq = tensor(mixer, "o_sq", [P, 2, TB, V_DIM])
            NCONV = 2
            conv_y = tensor(mixer, "conv_y", [P, NCONV, SEQ])
            conv_s = tensor(mixer, "conv_s", [P, NCONV, SEQ])
        x_res = tensor(ctx, "x_res", [P, TB, D])
        acc = tensor(ctx, "acc", [P, TB, D])
        g_post_mix = tensor(ctx, "g_post_mix", [P, D])
        g_post_mlp = tensor(ctx, "g_post_mlp", [P, D])
        a_sb = tensor(ctx, "a_sb", [P, TB, W])

        ps = ctx.enter_context(nc.psum_tensor("ps", [P, 8, W], F32))

        ident_landed, gains_landed = sem("ident_landed"), sem("gains_landed")
        tables_landed = sem("tables_landed")
        x_landed = [sem(f"x_landed{q}") for q in range(4)]
        raw_landed = [sem(f"raw_landed{i}") for i in range(RAW)]
        x_res_landed, g_mix_landed, g_mlp_landed = sem("x_res_landed"), sem("g_mix_landed"), sem("g_mlp_landed")
        out_landed = sem("out_landed")
        hi_ready, lo_ready, half_used = sem("hi_ready"), sem("lo_ready"), sem("half_used")
        ones_ready, gainsT_filled, gains_ready = sem("ones_ready"), sem("gainsT_filled"), sem("gains_ready")
        xT_filled, xT_hi_ready, xT_lo_ready = sem("xT_filled"), sem("xT_hi_ready"), sem("xT_lo_ready")
        ss_x_ready, rstd_x_ready = sem("ss_x_ready"), sem("rstd_x_ready")
        strip_out_act, strip_out_dve = sem("strip_out_act"), sem("strip_out_dve")
        ss_lat_ready, rstd_lat_ready, lat_ready = sem("ss_lat_ready"), sem("rstd_lat_ready"), sem("lat_ready")
        latT_filled, latT_hi_ready, latT_lo_ready = sem("latT_filled"), sem("latT_hi_ready"), sem("latT_lo_ready")
        kr_ready, krT_filled, krT_ready = sem("kr_ready"), sem("krT_filled"), sem("krT_ready")
        kv0_ready, kv1_ready = sem("kv0_ready"), sem("kv1_ready")
        q_ready, q_rope_ready = sem("q_ready"), sem("q_rope_ready")
        kT_filled, kT_ready = sem("kT_filled"), sem("kT_ready")
        qT_filled, qT_ready = sem("qT_filled"), sem("qT_ready")
        qrT_filled, qrT_ready = sem("qrT_filled"), sem("qrT_ready")
        scores_done, neg_max_ready, probs_ready = sem("scores_done"), sem("neg_max_ready"), sem("probs_ready")
        probsT_filled, probsT0_ready, probsT1_ready = sem("probsT_filled"), sem("probsT0_ready"), sem("probsT1_ready")
        pv_done, o_ready, o_sq_ready = sem("pv_done"), sem("o_ready"), sem("o_sq_ready")
        ss_o_ready, rstd_o_ready, o_normed = sem("ss_o_ready"), sem("rstd_o_ready"), sem("o_normed")
        oT_filled, oT_hi_ready, oT_lo_ready = sem("oT_filled"), sem("oT_hi_ready"), sem("oT_lo_ready")
        convT_filled, tap_ready, conv_y_ready = sem("convT_filled"), sem("tap_ready"), sem("conv_y_ready")
        conv_sq_ready, conv_sum_done, conv_std_ready = sem("conv_sq_ready"), sem("conv_sum_done"), sem("conv_std_ready")
        convT_ready = sem("convT_ready")
        y_squared, y_out, ss_y_ready, rstd_y_ready = sem("y_squared"), sem("y_out"), sem("ss_y_ready"), sem("rstd_y_ready")
        x2_ready, hT_filled, hT_hi_ready, hT_lo_ready = sem("x2_ready"), sem("hT_filled"), sem("hT_hi_ready"), sem("hT_lo_ready")
        ss_x2_ready, rstd_x2_ready = sem("ss_x2_ready"), sem("rstd_x2_ready")
        relu_ready, a_ready = sem("relu_ready"), sem("a_ready")
        aT_filled, aT_hi_ready, aT_lo_ready = sem("aT_filled"), sem("aT_hi_ready"), sem("aT_lo_ready")
        acc_added = sem("acc_added")
        m_squared, m_gained, ss_m_ready, rstd_m_ready = sem("m_squared"), sem("m_gained"), sem("ss_m_ready"), sem("rstd_m_ready")
        result_ready = sem("result_ready")
        dve_own, act_own, pool_own = sem("dve_own"), sem("act_own"), sem("pool_own")

        w_in, w_uq, w_ukv, w_o, w_up, w_down = (t[n][0] for n in ("w_in", "w_uq", "w_ukv", "w_o", "w_up", "w_down"))
        x_dram = t["x"][0].rearrange("(b p) d -> p b d", p=P)
        out_dram = out[0].rearrange("(b p) d -> p b d", p=P)

        def rows(w, k0, nk, cols):
            return w[k0 * P:(k0 + nk) * P, cols].rearrange("(c p) n -> p c n", p=P)

        def quad_source(n):
            z = quads[n]
            if z["kind"] == "in":
                return rows(w_in, 4 * z["q"], 4, slice(z["col"], z["col"] + z["width"]))
            if z["kind"] == "kv":
                return rows(w_ukv, 0, 4, slice(z["p"] * W, (z["p"] + 1) * W))
            if z["kind"] == "q":
                return rows(w_uq, 3 * z["part"], 3, slice(z["p"] * QW, (z["p"] + 1) * QW))
            if z["kind"] == "out":
                return rows(w_o, 4 * z["q"], 4, slice(z["col"], z["col"] + W))
            return rows(w_up, 4 * z["q"], 4, slice(0, W))

        def half_shape(h):
            if h // 2 >= NQ:
                return (h % 2) * 2 * W, 2 * W
            z = quads[h // 2]
            first = 2 * z["width"] * (h % 2)
            return first, z["width"] * min(2, z["nk"] - 2 * (h % 2))

        def chunk_of(n, k, width):
            slot = (2 * n + k // 2) % AHEAD
            cols = slice((k % 2) * width, (k % 2 + 1) * width)
            return w_hi[:, slot, cols], w_lo[:, slot, cols]

        def blocks(tile, k, tb):
            return tile[:, k, tb * P:(tb + 1) * P]

        def f32(ap):
            return ap.bitcast(F32)

        X_BANK = [2 + j % 6 for j in range(8)]
        LAT_BANK = [4, 5, 7, 4, 5]
        LAT_CHUNK = [("kv", 0), ("kv", 2), ("q", 0), ("q", 2), ("q", 4)]

        def lat_cols(j, c):
            kind, k = LAT_CHUNK[j]
            return (0 if kind == "q" else Q_RANK) + (k + c) * P

        def latT_dst(j, c):
            kind, k = LAT_CHUNK[j]
            if kind == "q":
                return cqT_hi[:, k + c, :], cqT_lo[:, k + c, :], G_Q + k + c
            return yT_hi[:, KV_AT + k + c, :], yT_lo[:, KV_AT + k + c, :], G_KV + k + c

        def conv_bank(half, c):
            return 7 if half == 0 else 4 + c

        def wait_kv_buffers(eng, p):
            if p >= 1:
                eng.wait_ge(kT_filled, p)
            if p >= 2:
                eng.wait_ge(pv_done, p - 1)

        block = ctx.enter_context(nc.Block())

        @block.sync
        def _(sp):
            def load_quad(slot, source, nk=4, width=W):
                dst = raw[:, slot, 0:nk * width].rearrange("p (c n) -> p c n", c=nk)
                sp.dma_start(dst, source).then_inc(raw_landed[slot], 16)

            sp.dma_start(ident[:], t["ident"]).then_inc(ident_landed, 16)
            row = 0
            for name, n in [("pre_mix_g", 16), ("pre_mlp_g", 16), ("q_norm_g", 6), ("kv_norm_g", 4),
                            ("conv_out_g", 8), ("attn_out_g", 8)]:
                sp.dma_start(gain_rows[row:row + n, :],
                             t[name][0].rearrange("(k p) -> k p", p=P)).then_inc(gains_landed, 16)
                row += n
            sp.dma_start(gain_rows[row:G_ROWS, :],
                         t["conv_w"][0].rearrange("j (k p) -> (j k) p", p=P)).then_inc(gains_landed, 16)
            for q in range(4):
                cols = slice(q * W, (q + 1) * W)
                sp.dma_start(x_in[:, :, cols], x_dram[:, :, cols]).then_inc(x_landed[q], 16)
                load_quad(q, quad_source(q))
            sp.dma_start(cos_t[:], t["cos"]).then_inc(tables_landed, 16)
            sp.dma_start(sin_t[:], t["sin"]).then_inc(tables_landed, 16)
            for n in range(RAW, NQ):
                z = quads[n]
                sp.wait_ge(lo_ready, 2 * (n - RAW) + 2)
                load_quad(n % RAW, quad_source(n), z["nk"], z["width"])
                if n == NQ - 13:
                    sp.wait_ge(convT_ready, 8)
                    sp.wait_ge(oT_lo_ready, PAIRS)
                    sp.dma_start(g_post_mix[:], t["post_mix_g"].to_broadcast([P, D])).then_inc(g_mix_landed, 16)
                    sp.dma_start(x_res[:], x_dram).then_inc(x_res_landed, 16)
            with sp.Fori(1, FF_STRIPS) as j:
                for i in range(8):
                    sp.wait_ge(lo_ready, (j - 1) * 16 + 2 * (NQ + i - RAW) + 2)
                    if i < 4:
                        src = rows(w_up, 4 * i, 4, bass.ds(j * W, W))
                    else:
                        src = w_down[bass.ds((j - 1) * W, W), (i - 4) * W:(i - 3) * W].rearrange(
                            "(c p) n -> p c n", p=P)
                    load_quad(i % RAW, src)
            for i in range(4):
                sp.wait_ge(lo_ready, 2 * (NQ_ALL - 4 + i - RAW) + 2)
                load_quad(i, rows(w_down, 4 * (FF_STRIPS - 1), 4, slice(i * W, (i + 1) * W)))
            sp.dma_start(g_post_mlp[:], t["post_mlp_g"].to_broadcast([P, D])).then_inc(g_mlp_landed, 16)
            for q in range(4):
                sp.wait_ge(result_ready, q + 1)
                cols = slice(q * W, (q + 1) * W)
                sp.dma_start(out_dram[:, :, cols], x_res[:, :, cols]).then_inc(out_landed, 16)
            sp.wait_ge(out_landed, 64)

        @block.tensor
        def _(pe):
            def product(bank, width, lhs, k, wk, first, last):
                hi, lo = wk
                for tb in range(TB):
                    dst = ps[:, bank + tb, 0:width]
                    x_hi, x_lo = blocks(lhs[0], k, tb), blocks(lhs[1], k, tb)
                    nc.tensor.matmul(dst, x_hi, hi, start=first, stop=False)
                    nc.tensor.matmul(dst, x_lo, hi, start=False, stop=False)
                    mm = nc.tensor.matmul(dst, x_hi, lo, start=False, stop=last)
                return mm

            def transposes(bank, sources):
                for i, src in enumerate(sources):
                    mm = nc.tensor.transpose(ps[:, bank, i * P:(i + 1) * P], src, ident[:])
                return mm

            def strip_bank(strip):
                return 2 * (strip % 2)

            def wait_strip_bank(strip):
                s = strip - 2
                if s < 0:
                    return
                if s < S_OUT:
                    by_act = [1, 2, 3, 4, 0, 5, 6, 0, 7][s]
                    if by_act:
                        pe.wait_ge(strip_out_act, by_act)
                    else:
                        pe.wait_ge(strip_out_dve, 1 if s < 6 else 2)
                else:
                    pe.wait_ge(y_squared, 2 * (s - S_OUT) + 2)
                    pe.wait_ge(y_out, s - S_OUT + 1)

            def stream(n, k):
                z = quads[n]
                width, kind = z["width"], z["kind"]
                if k % 2 == 0:
                    pe.wait_ge(lo_ready, 2 * n + k // 2 + 1)
                wk = chunk_of(n, k, width)
                if kind == "in":
                    if z["first"] and k == 0:
                        wait_strip_bank(z["strip"])
                    if z["strip"] == 0 and k == 0:
                        pe.wait_ge(xT_lo_ready, 2 * z["q"] + 2)
                    first, last = z["first"] and k == 0, z["last"] and k == 3
                    mm = product(strip_bank(z["strip"]), width, (xT_hi, xT_lo), 4 * z["q"] + k, wk, first, last)
                elif kind == "out":
                    if z["first"] and k == 0:
                        wait_strip_bank(z["strip"])
                        if z["strip"] == S_OUT:
                            pe.wait_ge(oT_lo_ready, PAIRS)
                    if z["strip"] == S_OUT and z["q"] < 2 and k == 0:
                        pe.wait_ge(convT_ready, 4 * z["q"] + 4)
                    first, last = z["first"] and k == 0, z["last"] and k == 3
                    mm = product(strip_bank(z["strip"]), width, (yT_hi, yT_lo), 4 * z["q"] + k, wk, first, last)
                elif kind == "kv":
                    if k == 0:
                        if z["p"] == 0:
                            pe.wait_ge(latT_lo_ready, 5)
                        else:
                            pe.wait_ge(probs_ready, 2 * z["p"])
                            pe.wait_ge(probsT0_ready, z["p"])
                    last = k == 3
                    mm = product(4, width, (yT_hi, yT_lo), KV_AT + k, wk, k == 0, last)
                elif kind == "q":
                    if k == 0 and z["part"] == 0:
                        pe.wait_ge(kv0_ready, z["p"] + 1)
                        pe.wait_ge(kv1_ready, z["p"] + 1)
                    last = z["part"] == 1 and k == 2
                    mm = product(4, width, (cqT_hi, cqT_lo), 3 * z["part"] + k, wk,
                                 z["part"] == 0 and k == 0, last)
                else:
                    if k == 0:
                        pe.wait_ge(hT_lo_ready, 2 * z["q"] + 2)
                        if z["q"] == 0:
                            pe.wait_ge(y_squared, 8)
                            pe.wait_ge(y_out, 4)
                    last = z["last"] and k == 3
                    mm = product(0, width, (xT_hi, xT_lo), 4 * z["q"] + k, wk, z["first"] and k == 0, last)
                if k % 2 == 1 or k == z["nk"] - 1:
                    mm.then_inc(half_used, 1)

            pe.wait_ge(ident_landed, 16)
            pe.wait_ge(gains_landed, 16 * 7)
            nc.tensor.transpose(ps[:, 0, 0:G_ROWS], gain_rows[0:G_ROWS, :],
                                ident[0:G_ROWS, 0:G_ROWS]).then_inc(gainsT_filled, 1)

            def hidden_transposes(j):
                pe.wait_ge(a_ready, j + 1)
                for tb in range(TB):
                    mm = transposes(2 + tb, [a_sb[:, tb, c * P:(c + 1) * P] for c in range(4)])
                mm.then_inc(aT_filled, 1)

            def down_quad(i, half, added):
                pe.wait_ge(acc_added, added)
                for k in range(4):
                    if k % 2 == 0:
                        pe.wait_ge(lo_ready, half + k // 2 + 1)
                    mm = product(4 + 2 * (i % 2), W, (yT_hi, yT_lo), k, chunk_of(i, k, W), k == 0, k == 3)
                    if k % 2:
                        mm.then_inc(half_used, 1)

            for what, a, b in steps:
                if what == "mm":
                    stream(a, b)
                elif what == "xT":
                    pe.wait_ge(x_landed[a // 2], 16)
                    if a >= 6:
                        pe.wait_ge(xT_lo_ready, a - 5)
                    transposes(X_BANK[a], [x_in[:, tb, (2 * a + c) * P:(2 * a + c + 1) * P]
                                           for c in range(2) for tb in range(TB)]).then_inc(xT_filled, 1)
                elif what == "latT":
                    pe.wait_ge(lat_ready, 1)
                    if a >= 3:
                        pe.wait_ge(latT_lo_ready, a - 2)
                    transposes(LAT_BANK[a], [lat[:, tb, lat_cols(a, c):lat_cols(a, c) + P]
                                             for c in range(2) for tb in range(TB)]).then_inc(latT_filled, 1)
                elif what == "krT":
                    pe.wait_ge(kr_ready, 4)
                    transposes(6, [kr_rot[:, tb].rearrange("p e r -> p (e r)")
                                   for tb in range(TB)]).then_inc(krT_filled, 1)
                elif what == "kT":
                    pe.wait_ge(q_ready, a + 1)
                    pe.wait_ge(kv0_ready, a + 1)
                    pe.wait_ge(kv1_ready, a + 1)
                    transposes(4, [k_sb[:, tb, h] for h in range(2) for tb in range(TB)]).then_inc(kT_filled, 1)
                elif what == "qT":
                    pe.wait_ge(q_ready, a + 1)
                    transposes(5, [q_sb[:, tb, h * (NOPE + ROPE):h * (NOPE + ROPE) + NOPE]
                                   for h in range(2) for tb in range(TB)]).then_inc(qT_filled, 1)
                elif what == "qrT":
                    pe.wait_ge(q_rope_ready, 4 * (a + 1))
                    pe.wait_ge(kT_ready, a + 1)
                    transposes(4, [qr_rot[:, tb].rearrange("p e r -> p (e r)")
                                   for tb in range(TB)]).then_inc(qrT_filled, 1)
                elif what == "scores":
                    p, h = a, b
                    pe.wait_ge(kT_ready, p + 1)
                    pe.wait_ge(qT_ready, p + 1)
                    pe.wait_ge(qrT_ready, p + 1)
                    pe.wait_ge(krT_ready, 1)
                    if p and not h:
                        pe.wait_ge(oT_lo_ready, p)
                    bank, rp = (6, 4)[h], slice(ROPE * h, ROPE * (h + 1))
                    for tb, cols, keys in [(0, slice(0, P), slice(0, P)), (1, slice(P, 3 * P), slice(0, SEQ))]:
                        nc.tensor.matmul(ps[:, bank, cols], qT_sb[:, h, tb * P:(tb + 1) * P], kT_sb[:, h, keys],
                                         start=True, stop=False)
                        mm = nc.tensor.matmul(ps[:, bank, cols], qrT_sb[rp, tb * P:(tb + 1) * P], krT[rp, keys],
                                              start=False, stop=True)
                    mm.then_inc(scores_done, 1)
                elif what == "probsT":
                    pe.wait_ge(probs_ready, 2 * a + b + 1)
                    if b == 0:
                        pe.wait_ge(qT_ready, a + 1)
                    transposes((5, 6)[b], [probs[:, b, i * P:(i + 1) * P] for i in range(3)]
                               ).then_inc(probsT_filled, 1)
                elif what == "pv":
                    pe.wait_ge(kv0_ready, a + 1)
                    pe.wait_ge(kv1_ready, a + 1)
                    pe.wait_ge(probsT0_ready, a + 1)
                    pe.wait_ge(probsT1_ready, a + 1)
                    for h in range(2):
                        o = [ps[:, 6, (2 * h + tb) * P:(2 * h + tb + 1) * P] for tb in range(TB)]
                        v = [v_sb[:, a % 2, tb, h] for tb in range(TB)]
                        nc.tensor.matmul(o[0], probsT[:, h, 0:P], v[0], start=True, stop=True)
                        nc.tensor.matmul(o[1], probsT[:, h, P:2 * P], v[0], start=True, stop=False)
                        mm = nc.tensor.matmul(o[1], probsT[:, h, 2 * P:3 * P], v[1], start=False, stop=True)
                    mm.then_inc(pv_done, 1)
                elif what == "oT":
                    pe.wait_ge(o_normed, a + 1)
                    transposes(6, [o_sb[:, h, tb] for h in range(2) for tb in range(TB)]).then_inc(oT_filled, 1)
                elif what == "convT":
                    pe.wait_ge(strip_out_dve, a + 1)
                    pe.wait_ge(strip_out_act, (5, 7)[a])
                    if a:
                        pe.wait_ge(oT_lo_ready, PAIRS)
                        pe.wait_ge(conv_std_ready, 4)
                    elif b:
                        pe.wait_ge(conv_std_ready, b)
                    else:
                        pe.wait_ge(latT_lo_ready, 3)
                    transposes(conv_bank(a, b), [s[:, tb, b * P:(b + 1) * P] for s in (u_sb, b_sb)
                                                 for tb in range(TB)]).then_inc(convT_filled, 1)
                elif what == "conv_norm":
                    i = 4 * a + b
                    pe.wait_ge(ones_ready, 1)
                    pe.wait_ge(conv_sq_ready, i + 1)
                    nc.tensor.matmul(ps[:, conv_bank(a, b), 0:SEQ], ones[:], conv_s[:, i % NCONV, :],
                                     start=True, stop=True).then_inc(conv_sum_done, 1)
                elif what == "hT":
                    pe.wait_ge(x2_ready, a // 2 + 1)
                    if a >= 4:
                        pe.wait_ge(hT_lo_ready, a - 3)
                    transposes(4 + a % 4, [x_res[:, tb, (2 * a + c) * P:(2 * a + c + 1) * P]
                                           for c in range(2) for tb in range(TB)]).then_inc(hT_filled, 1)
                elif what == "aT":
                    hidden_transposes(a)


            with pe.Fori(1, FF_STRIPS) as j:
                base = (j - 1) * 16 + 2 * NQ
                pe.wait_ge(relu_ready, j)
                for i in range(4):
                    for k in range(4):
                        if k % 2 == 0:
                            pe.wait_ge(lo_ready, base + (2 * i + k // 2 + 1))
                        mm = product(0, W, (xT_hi, xT_lo), 4 * i + k, chunk_of(i, k, W),
                                     i == 0 and k == 0, i == 3 and k == 3)
                        if k % 2:
                            mm.then_inc(half_used, 1)
                pe.wait_ge(aT_lo_ready, j)
                for i in range(4):
                    down_quad(i, base + (8 + 2 * i), (j - 1) * 4 + (i + 1))
                hidden_transposes(j)
            pe.wait_ge(aT_lo_ready, FF_STRIPS)
            for i in range(4):
                down_quad(i, 2 * (NQ_ALL - 4 + i), 4 * (FF_STRIPS - 1) + i + 1)

        @block.scalar
        def _(act):
            def own(ins):
                own.count += 1
                ins.then_inc(act_own, 1)
                act.wait_ge(act_own, own.count)
            own.count = 0

            def split_hi(slot, raw_slot, first, size, used, landed):
                if used is not None:
                    act.wait_ge(half_used, used)
                act.wait_ge(raw_landed[raw_slot], landed)
                nc.scalar.activation(w_hi[:, slot, 0:size], raw[:, raw_slot, first:first + size],
                                     ACT.Copy).then_inc(hi_ready, 1)

            def split_static(h):
                n = h // 2
                first, size = half_shape(h)
                split_hi(h % AHEAD, n % RAW, first, size, h - AHEAD + 1 if h >= AHEAD else None,
                         16 * (n // RAW + 1))

            def scaled_out(dst, bank, width, scale):
                for tb in range(TB):
                    ins = nc.scalar.activation(dst[tb], ps[:, bank + tb, 0:width], ACT.Copy,
                                               scale=scale[:, tb:tb + 1])
                return ins

            def gained_hi(dst, bank, gain):
                for c in range(2):
                    ins = nc.scalar.activation(dst[c], ps[:, bank, c * SEQ:(c + 1) * SEQ], ACT.Copy,
                                               scale=gains[:, gain[c]:gain[c] + 1])
                return ins

            def relu_out(j, done):
                act.wait_ge(half_used, done)
                for tb in range(TB):
                    ins = nc.scalar.activation(a_sb[:, tb], ps[:, tb], ACT.Relu, scale=rstd_x2[:, tb:tb + 1])
                ins.then_inc(relu_ready, 1)

            def hidden_hi(j):
                act.wait_ge(aT_filled, j + 1)
                for tb in range(TB):
                    ins = nc.scalar.activation(yT_hi[:, 0:4, tb * P:(tb + 1) * P],
                                               ps[:, 2 + tb].rearrange("p (c t) -> p c t", c=4), ACT.Copy)
                ins.then_inc(aT_hi_ready, 1)

            for h in range(AHEAD):
                split_static(h)
            for what, a, b in steps:
                if what == "mm":
                    if b % 2 == 1 or b == quads[a]["nk"] - 1:
                        split_static(2 * a + b // 2 + AHEAD)
                elif what == "xT":
                    act.wait_ge(xT_filled, a + 1)
                    act.wait_ge(gains_ready, 1)
                    gained_hi([xT_hi[:, 2 * a + c] for c in range(2)], X_BANK[a],
                              [G_MIX + 2 * a + c for c in range(2)]).then_inc(xT_hi_ready, 1)
                elif what == "x_stats":
                    for q in range(4):
                        act.wait_ge(x_landed[q], 16)
                    for tb in range(TB):
                        if tb:
                            act.wait_ge(ss_x_ready, tb)
                        nc.scalar.activation(lat.rearrange("p b n -> p (b n)")[:, 0:D], x_in[:, tb], ACT.Square,
                                             accum_out=ss_x[:, tb:tb + 1]).then_inc(ss_x_ready, 1)
                elif what == "lat_out":
                    act.wait_ge(half_used, 2 * b + 2)
                    act.wait_ge(rstd_x_ready, 1)
                    if a == 0:
                        act.wait_ge(ss_x_ready, 2)
                    width = quads[b]["width"]
                    scaled_out([lat[:, tb, a * W:a * W + width] for tb in range(TB)], 2 * (a % 2), width,
                               rstd_x).then_inc(strip_out_act, 1)
                elif what == "lat_norm":
                    act.wait_ge(strip_out_act, 3)
                    for i, (c0, c1) in enumerate([(0, Q_RANK), (Q_RANK, Q_RANK + KV_RANK)]):
                        for tb in range(TB):
                            if i or tb:
                                act.wait_ge(ss_lat_ready, 2 * i + tb)
                            nc.scalar.activation(u_sb.rearrange("p b n -> p (b n)")[:, 0:c1 - c0],
                                                 lat[:, tb, c0:c1], ACT.Square,
                                                 accum_out=ss_lat[:, 2 * i + tb:2 * i + tb + 1]
                                                 ).then_inc(ss_lat_ready, 1)
                elif what == "latT":
                    act.wait_ge(latT_filled, a + 1)
                    dst = [latT_dst(a, c) for c in range(2)]
                    gained_hi([d[0] for d in dst], LAT_BANK[a], [d[2] for d in dst]).then_inc(latT_hi_ready, 1)
                elif what == "kv_out":
                    act.wait_ge(half_used, 2 * b + 2)
                    wait_kv_buffers(act, a)
                    kv = ps[:, 4].rearrange("p (h e n) -> p h e n", h=2, e=2)
                    nc.scalar.activation(k_sb[:, 0], kv[:, :, 0], ACT.Copy)
                    nc.scalar.activation(v_sb[:, a % 2, 0], kv[:, :, 1], ACT.Copy).then_inc(kv0_ready, 1)
                elif what == "q_out":
                    act.wait_ge(half_used, 2 * b + 2)
                    if a:
                        act.wait_ge(q_rope_ready, 4 * a)
                        act.wait_ge(qT_filled, a)
                    for tb in range(TB):
                        ins = nc.scalar.activation(q_sb[:, tb], ps[:, 4 + tb, 0:QW], ACT.Copy)
                    ins.then_inc(q_ready, 1)
                elif what == "qT":
                    act.wait_ge(qT_filled, a + 1)
                    if a:
                        act.wait_ge(scores_done, 2 * a)
                    nc.scalar.activation(qT_sb.rearrange("p h t -> p (h t)"), ps[:, 5],
                                         ACT.Copy).then_inc(qT_ready, 1)
                elif what == "scores":
                    i = 2 * a + b
                    act.wait_ge(neg_max_ready, i + 1)
                    if a:
                        act.wait_ge(probsT_filled, i - 1)
                    bank = (6, 4)[b]
                    for tb, cols in [(0, slice(0, P)), (1, slice(P, 3 * P))]:
                        s = 2 * b + tb
                        ins = nc.scalar.activation(probs[:, b, cols], ps[:, bank, cols], ACT.Exp, scale=SCALE,
                                                   bias=neg_max[:, s:s + 1], accum_out=row_sum[:, s:s + 1])
                    ins.then_inc(probs_ready, 1)
                elif what == "probsT" and b == 1:
                    act.wait_ge(probsT_filled, 2 * a + 2)
                    if a:
                        act.wait_ge(pv_done, a)
                    nc.scalar.activation(probsT[:, 1], ps[:, 6, 0:3 * P], ACT.Copy).then_inc(probsT1_ready, 1)
                elif what == "oT":
                    act.wait_ge(oT_filled, a + 1)
                    gained_hi([yT_hi[:, 8 + 2 * a + h] for h in range(2)], 6,
                              [G_ATT + 2 * a + h for h in range(2)]).then_inc(oT_hi_ready, 1)
                elif what == "conv_out" and CONV_PARTS[a] != "c":
                    act.wait_ge(half_used, 2 * b + 2)
                    if a >= 3:
                        act.wait_ge(convT_filled, 4)
                    elif CONV_PARTS[a] == "u":
                        act.wait_ge(ss_lat_ready, 4)
                    dst = u_sb if CONV_PARTS[a] == "u" else b_sb
                    scaled_out([dst[:, tb] for tb in range(TB)], 2 * ((S_CONV + a) % 2), W,
                               rstd_x).then_inc(strip_out_act, 1)
                elif what == "convT":
                    i = 4 * a + b
                    act.wait_ge(convT_filled, i + 1)
                    if i >= NCONV:
                        act.wait_ge(convT_ready, i - NCONV + 1)
                    tap = G_TAP + 2 * 8 + i
                    nc.scalar.activation(conv_y[:, i % NCONV], ps[:, conv_bank(a, b), 0:SEQ], ACT.Copy,
                                         scale=gains[:, tap:tap + 1]).then_inc(tap_ready, 1)
                elif what == "conv_square":
                    i = 4 * a + b
                    act.wait_ge(conv_y_ready, i + 1)
                    nc.scalar.activation(conv_s[:, i % NCONV], conv_y[:, i % NCONV],
                                         ACT.Square).then_inc(conv_sq_ready, 1)
                elif what == "conv_norm":
                    i = 4 * a + b
                    act.wait_ge(conv_sum_done, i + 1)
                    nc.scalar.activation(conv_s[:, i % NCONV], ps[:, conv_bank(a, b), 0:SEQ], ACT.Sqrt,
                                         scale=1.0 / P, bias=eps_col[:, 0:1]).then_inc(conv_std_ready, 1)
                elif what == "y_out":
                    act.wait_ge(half_used, 2 * b + 2)
                    if a:
                        act.wait_ge(y_squared, 2 * a)
                    for tb in range(TB):
                        nc.scalar.activation(a_sb[:, tb], ps[:, 2 * ((S_OUT + a) % 2) + tb], ACT.Square,
                                             accum_out=ss_strip[:, tb, a:a + 1]).then_inc(y_squared, 1)
                elif what == "hT":
                    act.wait_ge(hT_filled, a + 1)
                    gained_hi([xT_hi[:, 2 * a + c] for c in range(2)], 4 + a % 4,
                              [G_MLP + 2 * a + c for c in range(2)]).then_inc(hT_hi_ready, 1)
                elif what == "x2_stats":
                    act.wait_ge(x2_ready, 4)
                    for tb in range(TB):
                        nc.scalar.activation(acc[:, tb], x_res[:, tb], ACT.Square,
                                             accum_out=ss_x[:, tb:tb + 1]).then_inc(ss_x2_ready, 1)
                elif what == "relu":
                    act.wait_ge(rstd_x2_ready, 1)
                    relu_out(0, 2 * NQ)
                elif what == "aT":
                    hidden_hi(0)

            with act.Fori(1, FF_STRIPS) as j:
                base = (j - 1) * 16 + 2 * NQ
                for i in range(16):
                    if i == 7:
                        relu_out(j, base + 8)
                    split_hi(i % AHEAD, (i + AHEAD) // 2 % RAW, (i % 2) * 2 * W, 2 * W, base + (i + 1),
                             (j - 1) * 32 + 16 * ((2 * NQ + i + AHEAD) // (2 * RAW) + 1))
                hidden_hi(j)
            for i in range(4):
                if i < 2:
                    for h in (2 * i, 2 * i + 1):
                        split_static(2 * (NQ_ALL - 4) + h + AHEAD)
                act.wait_ge(acc_added, 4 * FF_STRIPS + i - 1)
                if i:
                    act.wait_ge(m_squared, i)
                for tb in range(TB):
                    ins = nc.scalar.activation(a_sb[:, tb], acc[:, tb, i * W:(i + 1) * W], ACT.Square,
                                               accum_out=ss_strip[:, tb, i:i + 1])
                ins.then_inc(m_squared, 1)

        @block.vector
        def _(dve):
            def own(ins):
                own.count += 1
                ins.then_inc(dve_own, 1)
                dve.wait_ge(dve_own, own.count)
            own.count = 0

            def split_lo(slot, raw_slot, first, size, ready):
                dve.wait_ge(hi_ready, ready)
                nc.vector.tensor_tensor(w_lo[:, slot, 0:size], raw[:, raw_slot, first:first + size],
                                        f32(w_hi[:, slot, 0:size]), ALU.subtract).then_inc(lo_ready, 1)

            def split_static(h):
                first, size = half_shape(h)
                split_lo(h % AHEAD, h // 2 % RAW, first, size, h + 1)

            def gained_lo(hi, lo, bank, gain):
                for c in range(2):
                    ins = nc.vector.scalar_tensor_tensor(
                        out=lo[c], in0=ps[:, bank, c * SEQ:(c + 1) * SEQ], scalar=gains[:, gain[c]:gain[c] + 1],
                        in1=f32(hi[c]), op0=ALU.mult, op1=ALU.subtract)
                return ins

            def hidden_lo(j):
                dve.wait_ge(aT_hi_ready, j + 1)
                for tb in range(TB):
                    ins = nc.vector.tensor_tensor(yT_lo[:, 0:4, tb * P:(tb + 1) * P],
                                                  ps[:, 2 + tb].rearrange("p (c t) -> p c t", c=4),
                                                  f32(yT_hi[:, 0:4, tb * P:(tb + 1) * P]), ALU.subtract)
                ins.then_inc(aT_lo_ready, 1)

            def add_down(i, done, added):
                dve.wait_ge(half_used, done)
                dve.wait_ge(acc_added, added)
                m = acc[:, :, i * W:(i + 1) * W]
                bank = 4 + 2 * (i % 2)
                nc.vector.tensor_tensor(m, m, ps[:, bank:bank + 2], ALU.add).then_inc(acc_added, 1)

            dve.wait_ge(gainsT_filled, 1)
            nc.vector.tensor_copy(gains[:], ps[:, 0, 0:G_ROWS]).then_inc(gains_ready, 1)
            dve.wait_ge(gains_ready, 1)
            for h in range(AHEAD):
                split_static(h)
            for what, a, b in steps:
                if what == "mm":
                    if b % 2 == 1 or b == quads[a]["nk"] - 1:
                        split_static(2 * a + b // 2 + AHEAD)
                elif what == "xT":
                    dve.wait_ge(xT_hi_ready, a + 1)
                    ks = [2 * a, 2 * a + 1]
                    gained_lo([xT_hi[:, k] for k in ks], [xT_lo[:, k] for k in ks], X_BANK[a],
                              [G_MIX + k for k in ks]).then_inc(xT_lo_ready, 1)
                elif what == "lat_norm":
                    dve.wait_ge(rstd_lat_ready, 1)
                    dve.wait_ge(strip_out_act, 3)
                    for i, (c0, c1) in enumerate([(0, Q_RANK), (Q_RANK, Q_RANK + KV_RANK)]):
                        for tb in range(TB):
                            ins = nc.vector.tensor_scalar(lat[:, tb, c0:c1], lat[:, tb, c0:c1],
                                                          rstd_lat[:, 2 * i + tb:2 * i + tb + 1], None, ALU.mult)
                    ins.then_inc(lat_ready, 1)
                elif what == "latT":
                    dve.wait_ge(latT_hi_ready, a + 1)
                    dst = [latT_dst(a, c) for c in range(2)]
                    gained_lo([d[0] for d in dst], [d[1] for d in dst], LAT_BANK[a],
                              [d[2] for d in dst]).then_inc(latT_lo_ready, 1)
                elif what == "krT":
                    dve.wait_ge(krT_filled, 1)
                    nc.vector.tensor_copy(krT[:], ps[:, 6, 0:SEQ]).then_inc(krT_ready, 1)
                elif what == "kv_out":
                    dve.wait_ge(half_used, 2 * b + 2)
                    wait_kv_buffers(dve, a)
                    kv = ps[:, 5].rearrange("p (h e n) -> p h e n", h=2, e=2)
                    nc.vector.tensor_copy(k_sb[:, 1], kv[:, :, 0])
                    nc.vector.tensor_copy(v_sb[:, a % 2, 1], kv[:, :, 1]).then_inc(kv1_ready, 1)
                elif what == "kT":
                    dve.wait_ge(kT_filled, a + 1)
                    if a:
                        dve.wait_ge(scores_done, 2 * a)
                    nc.vector.tensor_copy(kT_sb.rearrange("p h t -> p (h t)"), ps[:, 4]).then_inc(kT_ready, 1)
                elif what == "qrT":
                    dve.wait_ge(qrT_filled, a + 1)
                    nc.vector.tensor_copy(qrT_sb[:], ps[:, 4, 0:SEQ]).then_inc(qrT_ready, 1)
                elif what == "scores":
                    i, bank = 2 * a + b, (6, 4)[b]
                    dve.wait_ge(scores_done, i + 1)
                    if a:
                        dve.wait_ge(probs_ready, i - 1)
                    nc.vector.memset(ps[0:CHUNK, bank, CHUNK:P], MASKED)
                    own(nc.vector.memset(ps[0:CHUNK, bank, 2 * P + CHUNK:3 * P], MASKED))
                    s = 2 * b
                    nc.vector.reduce_max(row_max[:, s:s + 1], ps[:, bank, 0:P], AX_X)
                    own(nc.vector.reduce_max(row_max[:, s + 1:s + 2], ps[:, bank, P:3 * P], AX_X))
                    nc.vector.tensor_scalar(neg_max[:, s:s + 2], row_max[:, s:s + 2], -SCALE, None,
                                            ALU.mult).then_inc(neg_max_ready, 1)
                elif what == "probsT" and b == 0:
                    dve.wait_ge(probsT_filled, 2 * a + 1)
                    if a:
                        dve.wait_ge(pv_done, a)
                    nc.vector.tensor_copy(probsT[:, 0], ps[:, 5, 0:3 * P]).then_inc(probsT0_ready, 1)
                elif what == "pv":
                    dve.wait_ge(probs_ready, 2 * a + 2)
                    own(nc.vector.reciprocal(inv_sum[:], row_sum[:]))
                    dve.wait_ge(pv_done, a + 1)
                    if a:
                        dve.wait_ge(oT_filled, a)
                    nc.vector.tensor_tensor(o_sb.rearrange("p h b n -> p (h b) n"),
                                            ps[:, 6].rearrange("p (s n) -> p s n", n=V_DIM),
                                            inv_sum[:].unsqueeze(2).to_broadcast([P, 4, V_DIM]),
                                            ALU.mult).then_inc(o_ready, 1)
                elif what == "o_squares":
                    dve.wait_ge(o_sq_ready, a + 1)
                    nc.vector.reduce_sum(ss_o[:], o_sq.rearrange("p h b n -> p (h b) n"), AX_X
                                         ).then_inc(ss_o_ready, 1)
                elif what == "o_norm":
                    dve.wait_ge(rstd_o_ready, a + 1)
                    o = o_sb.rearrange("p h b n -> p (h b) n")
                    nc.vector.tensor_tensor(o, o, rstd_o[:].unsqueeze(2).to_broadcast([P, 4, V_DIM]),
                                            ALU.mult).then_inc(o_normed, 1)
                elif what == "oT":
                    dve.wait_ge(oT_hi_ready, a + 1)
                    ks = [8 + 2 * a, 9 + 2 * a]
                    gained_lo([yT_hi[:, k] for k in ks], [yT_lo[:, k] for k in ks], 6,
                              [G_ATT + 2 * a, G_ATT + 2 * a + 1]).then_inc(oT_lo_ready, 1)
                elif what == "conv_out" and CONV_PARTS[a] == "c":
                    dve.wait_ge(half_used, 2 * b + 2)
                    dve.wait_ge(strip_out_act, 4 if a < 3 else 6)
                    for tb in range(TB):
                        ins = nc.vector.scalar_tensor_tensor(
                            out=u_sb[:, tb], in0=ps[:, 2 * ((S_CONV + a) % 2) + tb], scalar=rstd_x[:, tb:tb + 1],
                            in1=u_sb[:, tb], op0=ALU.mult, op1=ALU.mult)
                    ins.then_inc(strip_out_dve, 1)
                elif what == "convT":
                    i = 4 * a + b
                    dve.wait_ge(tap_ready, i + 1)
                    y, bank = conv_y[:, i % NCONV], conv_bank(a, b)
                    for back in (1, 2):
                        tap = G_TAP + 8 * (2 - back) + i
                        own(nc.vector.scalar_tensor_tensor(
                            out=y[:, back:SEQ], in0=ps[:, bank, 0:SEQ - back], scalar=gains[:, tap:tap + 1],
                            in1=y[:, back:SEQ], op0=ALU.mult, op1=ALU.add))
                    nc.vector.tensor_tensor(y, y, ps[:, bank, SEQ:2 * SEQ], ALU.mult).then_inc(conv_y_ready, 1)
                elif what == "conv_norm":
                    i = 4 * a + b
                    y, s = conv_y[:, i % NCONV], conv_s[:, i % NCONV]
                    dve.wait_ge(conv_std_ready, i + 1)
                    own(nc.vector.reciprocal(s, s))
                    own(nc.vector.scalar_tensor_tensor(out=y, in0=y, scalar=gains[:, G_CONV + i:G_CONV + i + 1],
                                                       in1=s, op0=ALU.mult, op1=ALU.mult))
                    own(nc.vector.tensor_copy(yT_hi[:, i], y))
                    nc.vector.tensor_tensor(yT_lo[:, i], y, f32(yT_hi[:, i]), ALU.subtract
                                            ).then_inc(convT_ready, 1)
                elif what == "y_out":
                    dve.wait_ge(half_used, 2 * b + 2)
                    dve.wait_ge(g_mix_landed, 16)
                    for tb in range(TB):
                        dve.wait_ge(y_squared, 2 * a + tb + 1)
                        ins = nc.vector.tensor_tensor(
                            acc[:, tb, a * W:(a + 1) * W], ps[:, 2 * ((S_OUT + a) % 2) + tb],
                            g_post_mix[:, a * W:(a + 1) * W], ALU.mult)
                    ins.then_inc(y_out, 1)
                elif what == "y_norm":
                    dve.wait_ge(y_squared, 8)
                    nc.vector.reduce_sum(ss_row[:], ss_strip[:], AX_X).then_inc(ss_y_ready, 1)
                elif what == "x2":
                    dve.wait_ge(rstd_y_ready, 1)
                    dve.wait_ge(y_out, 4)
                    dve.wait_ge(x_res_landed, 16)
                    cols = slice(a * W, (a + 1) * W)
                    for tb in range(TB):
                        ins = nc.vector.scalar_tensor_tensor(
                            out=x_res[:, tb, cols], in0=acc[:, tb, cols], scalar=rstd_row[:, tb:tb + 1],
                            in1=x_res[:, tb, cols], op0=ALU.mult, op1=ALU.add)
                    ins.then_inc(x2_ready, 1)
                elif what == "hT":
                    dve.wait_ge(hT_hi_ready, a + 1)
                    ks = [2 * a, 2 * a + 1]
                    gained_lo([xT_hi[:, k] for k in ks], [xT_lo[:, k] for k in ks], 4 + a % 4,
                              [G_MLP + k for k in ks]).then_inc(hT_lo_ready, 1)
                elif what == "aT":
                    hidden_lo(0)

            with dve.Fori(1, FF_STRIPS) as j:
                base = (j - 1) * 16 + 2 * NQ
                for i in range(16):
                    if i >= 8 and i % 2:
                        add_down((i - 9) // 2, base + (i + 1), (j - 1) * 4 + ((i - 9) // 2 + 2))
                    split_lo(i % AHEAD, (i + AHEAD) // 2 % RAW, (i % 2) * 2 * W, 2 * W,
                             base + (i + AHEAD + 1))
                hidden_lo(j)
            for i in range(4):
                if i < 2:
                    for h in (2 * i, 2 * i + 1):
                        split_static(2 * (NQ_ALL - 4) + h + AHEAD)
                add_down(i, 2 * (NQ_ALL - 4 + i) + 2, 4 * (FF_STRIPS - 1) + i + 2)
            dve.wait_ge(m_squared, 4)
            nc.vector.reduce_sum(ss_row[:], ss_strip[:], AX_X).then_inc(ss_m_ready, 1)
            dve.wait_ge(g_mlp_landed, 16)
            dve.wait_ge(acc_added, 4 * FF_STRIPS + 2)
            for tb in range(TB):
                ins = nc.vector.tensor_tensor(acc[:, tb, 3 * W:], acc[:, tb, 3 * W:], g_post_mlp[:, 3 * W:],
                                              ALU.mult)
            own(ins)
            dve.wait_ge(rstd_m_ready, 1)
            for i in range(4):
                if i < 3:
                    dve.wait_ge(m_gained, 2 * (i + 1))
                cols = slice(i * W, (i + 1) * W)
                for tb in range(TB):
                    ins = nc.vector.scalar_tensor_tensor(
                        out=x_res[:, tb, cols], in0=acc[:, tb, cols], scalar=rstd_row[:, tb:tb + 1],
                        in1=x_res[:, tb, cols], op0=ALU.mult, op1=ALU.add)
                ins.then_inc(result_ready, 1)

        @block.gpsimd
        def _(pool):
            def own(ins):
                own.count += 1
                ins.then_inc(pool_own, 1)
                pool.wait_ge(pool_own, own.count)
            own.count = 0

            def rstd(dst, ss, parts, ready, norm):
                for cols, n in parts:
                    ins = nc.gpsimd.tensor_scalar(mean_sq[:, norm, cols], ss[:, cols], 1.0 / n, EPS, ALU.mult, ALU.add)
                own(ins)
                width = parts[-1][0].stop
                nc.gpsimd.tensor_tensor(dst[:, 0:width], mean_sq[:, norm, 0:width], neg_half[:, 0:width],
                                        ALU.pow).then_inc(ready, 1)

            def rotate(src, cos, sin, dsts, ready):
                n = src.shape[1]
                nc.gpsimd.tensor_tensor(rope_c[:, 0:n], src, cos, ALU.mult)
                own(nc.gpsimd.tensor_tensor(rope_s[:, 0:n], src, sin, ALU.mult))
                lo, hi = slice(0, ROPE // 2), slice(ROPE // 2, ROPE)
                for dst in dsts:
                    nc.gpsimd.tensor_tensor(dst[:, :, lo], rope_c[:, 0:n, lo], rope_s[:, 0:n, hi], ALU.add
                                            ).then_inc(ready, 1)
                    nc.gpsimd.tensor_tensor(dst[:, :, hi], rope_c[:, 0:n, hi], rope_s[:, 0:n, lo], ALU.add
                                            ).then_inc(ready, 1)

            def square(j):
                pool.wait_ge(relu_ready, j + 1)
                a = a_sb.rearrange("p b n -> p (b n)")
                nc.gpsimd.tensor_tensor(a, a, a, ALU.mult).then_inc(a_ready, 1)

            def gain(i):
                pool.wait_ge(m_squared, i + 1)
                pool.wait_ge(g_mlp_landed, 16)
                cols = slice(i * W, (i + 1) * W)
                for tb in range(TB):
                    nc.gpsimd.tensor_tensor(acc[:, tb, cols], acc[:, tb, cols], g_post_mlp[:, cols], ALU.mult
                                            ).then_inc(m_gained, 1)

            nc.gpsimd.memset(eps_col[:], EPS)
            nc.gpsimd.memset(ones[:], 1.0).then_inc(ones_ready, 1)
            own(nc.gpsimd.memset(neg_half[:], -0.5))
            for what, a, b in steps:
                if what == "x_stats":
                    pool.wait_ge(ss_x_ready, 2)
                    rstd(rstd_x, ss_x, [(slice(0, 2), D)], rstd_x_ready, 0)
                elif what == "lat_norm":
                    pool.wait_ge(ss_lat_ready, 4)
                    rstd(rstd_lat, ss_lat, [(slice(0, 2), Q_RANK), (slice(2, 4), KV_RANK)], rstd_lat_ready, 1)
                    pool.wait_ge(tables_landed, 32)
                    pool.wait_ge(strip_out_act, 3)
                    rotate(lat[:, :, Q_RANK + KV_RANK:LAT], cos_t[:, :, 0:ROPE], sin_t[:, :, 0:ROPE],
                           [kr_rot[:, :, 0], kr_rot[:, :, 1]], kr_ready)
                elif what == "q_out":
                    pool.wait_ge(q_ready, a + 1)
                    if a:
                        pool.wait_ge(qrT_filled, a)
                    for tb in range(TB):
                        if a or tb:
                            pool.wait_ge(q_rope_ready, 4 * a + 2 * tb)
                        else:
                            pool.wait_ge(kr_ready, 4)
                        rotate(q_sb[:, tb].rearrange("p (h n) -> p h n", h=2)[:, :, NOPE:],
                               cos_t[:, tb].rearrange("p (h n) -> p h n", h=2),
                               sin_t[:, tb].rearrange("p (h n) -> p h n", h=2), [qr_rot[:, tb]], q_rope_ready)
                elif what == "pv":
                    pool.wait_ge(o_ready, a + 1)
                    if a:
                        pool.wait_ge(ss_o_ready, a)
                    nc.gpsimd.tensor_tensor(o_sq.rearrange("p h b n -> p (h b n)"),
                                            o_sb.rearrange("p h b n -> p (h b n)"),
                                            o_sb.rearrange("p h b n -> p (h b n)"), ALU.mult
                                            ).then_inc(o_sq_ready, 1)
                elif what == "o_squares":
                    pool.wait_ge(ss_o_ready, a + 1)
                    if a:
                        pool.wait_ge(rstd_o_ready, a)
                    rstd(rstd_o, ss_o, [(slice(0, 4), V_DIM)], rstd_o_ready, 2)
                elif what == "y_norm":
                    pool.wait_ge(ss_y_ready, 1)
                    rstd(rstd_row, ss_row, [(slice(0, 2), D)], rstd_y_ready, 3)
                elif what == "x2_stats":
                    pool.wait_ge(ss_x2_ready, 2)
                    rstd(rstd_x2, ss_x, [(slice(0, 2), D)], rstd_x2_ready, 4)
                    for tb in range(TB):
                        nc.gpsimd.memset(acc[:, tb], 0.0).then_inc(acc_added, 1)
                elif what == "relu":
                    square(0)

            with pool.Fori(1, FF_STRIPS) as j:
                square(j)
            for i in range(3):
                gain(i)
            pool.wait_ge(ss_m_ready, 1)
            rstd(rstd_row, ss_row, [(slice(0, 2), D)], rstd_m_ready, 5)


_INS = ["x", "pre_mix_g", "w_in", "conv_w", "q_norm_g", "w_uq", "kv_norm_g", "w_ukv", "conv_out_g",
        "attn_out_g", "w_o", "post_mix_g", "pre_mlp_g", "w_up", "w_down", "post_mlp_g"]
ROPE_THETA = 10000.0


def rope_tables():
    import numpy as np

    inv_freq = np.power(np.float32(ROPE_THETA), -np.arange(0, ROPE, 2, dtype=np.float32) / np.float32(ROPE))
    ang = np.arange(SEQ, dtype=np.float32)[:, None] * inv_freq.astype(np.float32)[None, :]
    cos, sin = np.cos(ang).astype(np.float32), np.sin(ang).astype(np.float32)
    tables = [np.concatenate([cos, cos, cos, cos], 1), np.concatenate([sin, -sin, sin, -sin], 1)]
    return [np.ascontiguousarray(a.reshape(TB, P, 2 * ROPE).transpose(1, 0, 2)) for a in tables]


def kernel(**inputs):
    import numpy as np
    import concourse.bacc as bacc
    from concourse.bass_utils import run_bass_kernel_spmd

    nc = bacc.Bacc("TRN2", target_bir_lowering=False, num_devices=1)
    arrays = {name: np.ascontiguousarray(inputs[name]) for name in _INS}
    arrays["cos"], arrays["sin"] = rope_tables()
    arrays["ident"] = np.eye(P, dtype=np.float32)
    arrays = {f"in_{name}": a for name, a in arrays.items()}
    t = {name[3:]: nc.dram_tensor(name, a.shape, mybir.dt.from_np(a.dtype), kind="ExternalInput").ap()
         for name, a in arrays.items()}
    out = nc.dram_tensor("out_dram", (1, SEQ, D), F32, kind="ExternalOutput").ap()
    hybrid_block(nc, t, out)
    result = run_bass_kernel_spmd(nc, [arrays], core_ids=[0])
    return result.results[0]["out_dram"]
```

```python
from contextlib import ExitStack

import concourse.bass as bass
from concourse import mybir

F32 = mybir.dt.float32
F32R = mybir.dt.float32r
ALU = mybir.AluOpType
ACT = mybir.ActivationFunctionType
AX_X = mybir.AxisListType.X

P = 128
SEQ = 256
TB = SEQ // P
D = 2048
CW = 1024
N_HEADS = 8
NOPE = 128
ROPE = 64
V_DIM = 128
Q_RANK = 768
KV_RANK = 512
D_FF = 8192
CHUNK = 64
EPS = 1e-6
SCALE = float(NOPE + ROPE) ** -0.5
MASKED = -1e30

W = 512
KC = D // P
LAT = Q_RANK + KV_RANK + ROPE
LAT0 = 3 * CW
PAIRS = N_HEADS // 2
QW = 2 * (NOPE + ROPE)
FF_STRIPS = D_FF // W
WARM_UP = 10
X_PARTS = [(0, 256), (256, 512), (512, 1024), (1024, 1536), (1536, 2048)]
RAW = 4
AHEAD = 4

G_MIX, G_MLP, G_Q, G_KV, G_CONV, G_ATT, G_TAP = 0, 16, 32, 38, 42, 50, 58
G_ROWS = G_TAP + 3 * (CW // P)

S_CONV, S_OUT = 3, 9
CONV_PARTS = "ucb" * 2


def plan():
    steps, tail, quads = [], [], {}

    def quad(kind, n=None, **kw):
        n = len(quads) if n is None else n
        quads[n] = dict(kind=kind, **kw)
        return n

    def products(n, into=steps, then=None):
        for k in range(quads[n]["nk"]):
            into.append(("mm", n, k))
            if k == 0 and then:
                into.extend(then)

    steps += [("split", 0, 0), ("xT", 0, 0), ("xT", 1, 0), ("split", 1, 0)]
    ahead = [[("xT", 2, 0), ("xT", 3, 0), ("split", 2, 0), ("split", 3, 0)],
             [("xT", 4, 0), ("xT", 5, 0)], [("xT", 6, 0), ("xT", 7, 0)], [("x_stats", 0, 0)]]
    for s in range(3):
        for q in range(4):
            n = quad("in", strip=s, q=q, nk=4, width=min(W, LAT - s * W), col=LAT0 + s * W,
                     first=q == 0, last=q == 3)
            products(n, then=ahead[q] if s == 0 else None)
        steps.append(("lat_out", s, n))
    steps.append(("lat_norm", 0, 0))

    def between(sub):
        if sub == 7:
            steps.extend([("latT", 0, 0), ("latT", 1, 0), ("krT", 0, 0), ("latT", 2, 0)])
        if sub == 10:
            steps.extend([("latT", 3, 0), ("latT", 4, 0)])
        for p in range(PAIRS):
            at = sub - 16 - 16 * p
            if at == 0:
                n = quad("kv", p=p, nk=4, width=W)
                products(n)
                steps.append(("kv_out", p, n))
            if at == 4:
                for part in range(2):
                    n = quad("q", p=p, part=part, nk=3, width=QW)
                    products(n)
                steps.append(("q_out", p, n))
            for when, what, h in [(6, "kT", 0), (7, "qT", 0), (9, "qrT", 0), (11, "scores", 0),
                                  (12, "scores", 1), (13, "probsT", 0), (15, "probsT", 1), (18, "pv", 0),
                                  (20, "o_squares", 0), (21, "o_norm", 0), (25, "oT", 0)]:
                if at == when:
                    steps.append((what, p, h))
        for c in range(4):
            for half, t in [(0, 77 + 6 * c), (1, 98 + 4 * c)]:
                if sub == t:
                    steps.append(("convT", half, c))
                if sub == t + 2:
                    steps.append(("conv_square", half, c))
                if sub == t + 5:
                    steps.append(("conv_norm", half, c))

    sub = 0
    for i, part in enumerate(CONV_PARTS):
        col = CW * "ubc".index(part) + W * (i // 3)
        for q in range(4):
            between(sub)
            n = quad("in", strip=S_CONV + i, q=q, nk=4, width=W, col=col, first=q == 0, last=q == 3)
            for k in range(4):
                if k:
                    between(sub)
                steps.append(("mm", n, k))
                sub += 1
        steps.append(("conv_out", i, n))

    order = [(0, 2), (0, 3), (0, 0), (1, 2), (1, 3), (1, 0), (0, 1), (1, 1)]
    order += [(s, q) for s in (2, 3) for q in (2, 3, 0, 1)]
    for s, q in order:
        n = quad("out", strip=S_OUT + s, q=q, nk=4, width=W, col=s * W, first=q == 2, last=q == 1)
        if s == 3 and q < 2:
            continue
        between(sub)
        for k in range(4):
            if k:
                between(sub)
            steps.append(("mm", n, k))
            sub += 1
        if q == 1:
            steps.append(("y_out", s, n))

    def up(j, q, n=None):
        return quad("up", n, j=j, q=q, nk=4, width=W)

    def down(j, q, n=None):
        return quad("down", n, j=j, q=q, nk=4, width=W)

    def mm_blocks(which, n, ks=range(4)):
        steps.extend((which, n, k) for k in ks)

    o0, o1 = n - 1, n
    u0, u1 = up(0, 0), up(0, 1)
    steps += [("y_partial", 0, 0)]
    mm_blocks("mm_b0", o0)
    mm_blocks("mm_b0", o1)
    steps += [("y_block", 0, 0), ("x2", 0, 0), ("x2", 1, 0), ("y_last", 0, 0)]
    mm_blocks("mm_b1", o0, (0, 1, 2))
    steps += [("h_split", 0, 0)]
    mm_blocks("mm_b1", o0, (3,))
    steps += [("hT", 0, 0)]
    mm_blocks("mm_b1", o1, (0, 1))
    steps += [("hT", 1, 0), ("h_split", 1, 0)]
    mm_blocks("mm_b1", o1, (2,))
    steps += [("y_block", 1, o1), ("x2", 2, 0)]
    mm_blocks("mm_b1", o1, (3,))
    steps += [("x2", 3, 0), ("x2", 4, 0), ("x2", 5, 0), ("y_last", 1, 0)]
    mm_blocks("mm_b0", u0)
    mm_blocks("mm_b0", u1, (0,))
    steps += [("hT", 2, 0), ("h_split", 2, 0)]
    mm_blocks("mm_b0", u1, (1, 2))
    steps += [("hT", 3, 0), ("h_split", 3, 0)]
    mm_blocks("mm_b0", u1, (3,))
    steps += [("x2", 6, 0), ("x2", 7, 0)]
    mm_blocks("mm_b1", u0, (0,))
    steps += [("hT", 4, 0), ("h_split", 4, 0), ("hT", 5, 0), ("h_split", 5, 0)]
    mm_blocks("mm_b1", u0, (1, 2, 3))
    mm_blocks("mm_b1", u1)

    u2 = up(0, 2)
    steps += [("mm", u2, 0), ("hT", 6, 0), ("h_split", 6, 0), ("mm", u2, 1), ("hT", 7, 0), ("h_split", 7, 0),
              ("mm", u2, 2), ("mm", u2, 3)]
    n = up(0, 3)
    products(n, then=[("x2_stats", 0, 0)])
    steps.append(("relu", 0, n))
    for q in range(4):
        n = up(1, q)
        products(n)
        if q == 1:
            steps.append(("aT", 0, 0))
    steps.append(("relu", 1, n))
    for q in range(4):
        n = down(0, q)
        products(n)
        steps.append(("add", q, n))
    steps.append(("aT", 1, 0))
    j = FF_STRIPS - 1
    n = len(quads) + 8 * (FF_STRIPS - 3) - 1
    for q in range(4):
        products(up(j, q, n := n + 1), tail)
    tail.append(("relu", j, n))
    for q in range(4):
        products(down(j - 1, q, n := n + 1), tail)
        tail.append(("add", 4 * (j - 1) + q, n))
        if q == 1:
            tail.append(("aT", j, 4))
    for q in range(2):
        n = down(j, q, n + 1)
        for k in range(4):
            if k == 3:
                tail.append(("add", 4 * j + q, n))
            tail.append(("mm", n, k))
            if q == 1 and k == 1:
                tail.append(("m_square", 0, 0))
    tail.append(("m_square", 1, 0))
    d2, d3 = down(j, 2, n + 1), down(j, 3, n + 2)
    for tb in range(TB):
        for q, n in [(2, d2), (3, d3)]:
            tail.extend((f"mm_b{tb}", n, k) for k in range(4))
            tail.append((f"m_add_b{tb}", q, n))
    return steps, tail, quads


def hybrid_block(nc, t, out):
    steps, tail, quads = plan()
    NQ_TAIL = min(n for what, n, _ in tail if what == "mm")
    NQ_ALL = max(quads) + 1
    LOOP = range(2, FF_STRIPS - 1)
    NQ = NQ_TAIL - 8 * len(LOOP)
    assert NQ % RAW == 0 and (2 * NQ) % AHEAD == 0

    with ExitStack() as ctx:
        def sem(name):
            return ctx.enter_context(nc.semaphore(name))

        def tensor(stack, name, shape, dt=F32):
            return stack.enter_context(nc.sbuf_tensor(name, shape, dt))

        ident = tensor(ctx, "ident", [P, P])
        ones = tensor(ctx, "ones", [P, P])
        gains = tensor(ctx, "gains", [P, G_ROWS])
        neg_half = tensor(ctx, "neg_half", [P, 4])
        ss_x = tensor(ctx, "ss_x", [P, TB])
        rstd_x = tensor(ctx, "rstd_x", [P, TB])
        rstd_x2 = tensor(ctx, "rstd_x2", [P, TB])
        ss_lat = tensor(ctx, "ss_lat", [P, 4])
        rstd_lat = tensor(ctx, "rstd_lat", [P, 4])
        row_max = tensor(ctx, "row_max", [P, 4])
        neg_max = tensor(ctx, "neg_max", [P, 4])
        row_sum = tensor(ctx, "row_sum", [P, 4])
        inv_sum = tensor(ctx, "inv_sum", [P, 4])
        ss_o = tensor(ctx, "ss_o", [P, 4])
        rstd_o = tensor(ctx, "rstd_o", [P, 4])
        ss_strip = tensor(ctx, "ss_strip", [P, TB, 4])
        ss_row = tensor(ctx, "ss_row", [P, TB])
        rstd_row = tensor(ctx, "rstd_row", [P, TB])
        rstd_m = tensor(ctx, "rstd_m", [P, TB])
        mean_sq = tensor(ctx, "mean_sq", [P, 8, 4])
        eps_col = tensor(ctx, "eps_col", [P, 1])
        xT_hi = tensor(ctx, "xT_hi", [P, KC, SEQ], F32R)
        xT_lo = tensor(ctx, "xT_lo", [P, KC, SEQ], F32R)
        yT_hi = tensor(ctx, "yT_hi", [P, KC, SEQ], F32R)
        yT_lo = tensor(ctx, "yT_lo", [P, KC, SEQ], F32R)
        raw = tensor(ctx, "raw", [P, RAW, 4 * W])
        w_hi = tensor(ctx, "w_hi", [P, AHEAD, 2 * W], F32R)
        w_lo = tensor(ctx, "w_lo", [P, AHEAD, 2 * W], F32R)
        KV_AT = 4
        with ExitStack() as mixer:
            cqT_hi = tensor(mixer, "cqT_hi", [P, Q_RANK // P, SEQ], F32R)
            cqT_lo = tensor(mixer, "cqT_lo", [P, Q_RANK // P, SEQ], F32R)
            lat = tensor(mixer, "lat", [P, TB, LAT])
            krT = tensor(mixer, "krT", [P, SEQ])
            kr_rot = tensor(mixer, "kr_rot", [P, TB, 2, ROPE])
            cos_t = tensor(mixer, "cos_t", [P, TB, 2 * ROPE])
            sin_t = tensor(mixer, "sin_t", [P, TB, 2 * ROPE])
            rope_c = tensor(mixer, "rope_c", [P, 2, ROPE])
            rope_s = tensor(mixer, "rope_s", [P, 2, ROPE])
            with ExitStack() as early:
                x_in = tensor(early, "x_in", [P, TB, D])
            u_sb = tensor(mixer, "u_sb", [P, 2, TB, W])
            b_sb = tensor(mixer, "b_sb", [P, 2, TB, W])
            q_sb = tensor(mixer, "q_sb", [P, TB, QW])
            qr_rot = tensor(mixer, "qr_rot", [P, TB, 2, ROPE])
            k_sb = tensor(mixer, "k_sb", [P, TB, 2, NOPE])
            v_sb = tensor(mixer, "v_sb", [P, 2, TB, 2, V_DIM])
            kT_sb = tensor(mixer, "kT_sb", [P, 2, SEQ])
            qT_sb = tensor(mixer, "qT_sb", [P, 2, SEQ])
            qrT_sb = tensor(mixer, "qrT_sb", [P, SEQ])
            probs = tensor(mixer, "probs", [P, 2, 3 * P])
            probsT = tensor(mixer, "probsT_sb", [P, 2, 3 * P])
            o_sb = tensor(mixer, "o_sb", [P, 2, TB, V_DIM])
            o_sq = tensor(mixer, "o_sq", [P, 2, TB, V_DIM])
            NCONV = 2
            conv_y = tensor(mixer, "conv_y", [P, NCONV, SEQ])
            conv_s = tensor(mixer, "conv_s", [P, NCONV, SEQ])
        x_res = tensor(ctx, "x_res", [P, TB, D])
        g_post_mix = tensor(ctx, "g_post_mix", [P, D])
        acc = tensor(ctx, "acc", [P, TB, D])
        g_post_mlp = tensor(ctx, "g_post_mlp", [P, D])
        a_sb = tensor(ctx, "a_sb", [P, TB, W])
        gained = tensor(ctx, "gained", [P, TB, W])

        ps = ctx.enter_context(nc.psum_tensor("ps", [P, 8, W], F32))

        ident_landed, gains_landed = sem("ident_landed"), sem("gains_landed")
        first_half_landed = sem("first_half_landed")
        tables_landed = sem("tables_landed")
        x_landed = [sem(f"x_landed{part}") for part in range(len(X_PARTS))]
        raw_landed = [sem(f"raw_landed{i}") for i in range(RAW)]
        x_res_landed, g_mix_landed, g_mlp_landed = sem("x_res_landed"), sem("g_mix_landed"), sem("g_mlp_landed")
        out_landed = sem("out_landed")
        hi_ready, lo_ready, half_used = sem("hi_ready"), sem("lo_ready"), sem("half_used")
        ones_ready = sem("ones_ready")
        xT_filled, xT_hi_ready, xT_lo_ready = sem("xT_filled"), sem("xT_hi_ready"), sem("xT_lo_ready")
        ss_x_ready, rstd_x_ready = sem("ss_x_ready"), sem("rstd_x_ready")
        strip_out_act, strip_out_dve = sem("strip_out_act"), sem("strip_out_dve")
        ss_lat_ready, rstd_lat_ready, lat_ready = sem("ss_lat_ready"), sem("rstd_lat_ready"), sem("lat_ready")
        latT_filled, latT_hi_ready, latT_lo_ready = sem("latT_filled"), sem("latT_hi_ready"), sem("latT_lo_ready")
        kr_ready, krT_filled, krT_ready = sem("kr_ready"), sem("krT_filled"), sem("krT_ready")
        kv0_ready, kv1_ready = sem("kv0_ready"), sem("kv1_ready")
        q_ready, q_rope_ready = sem("q_ready"), sem("q_rope_ready")
        kT_filled, kT_ready = sem("kT_filled"), sem("kT_ready")
        qT_filled, qT_ready = sem("qT_filled"), sem("qT_ready")
        qrT_filled, qrT_ready = sem("qrT_filled"), sem("qrT_ready")
        scores_done, neg_max_ready, probs_ready = sem("scores_done"), sem("neg_max_ready"), sem("probs_ready")
        probsT_filled, probsT0_ready, probsT1_ready = sem("probsT_filled"), sem("probsT0_ready"), sem("probsT1_ready")
        pv_done, o_ready, o_sq_ready = sem("pv_done"), sem("o_ready"), sem("o_sq_ready")
        ss_o_ready, rstd_o_ready, o_normed = sem("ss_o_ready"), sem("rstd_o_ready"), sem("o_normed")
        oT_filled, oT_hi_ready, oT_lo_ready = sem("oT_filled"), sem("oT_hi_ready"), sem("oT_lo_ready")
        convT_filled, tap_ready, conv_y_ready = sem("convT_filled"), sem("tap_ready"), sem("conv_y_ready")
        conv_sq_ready, conv_sum_done = sem("conv_sq_ready"), sem("conv_sum_done")
        conv_std_ready = sem("conv_std_ready")
        convT_ready = sem("convT_ready")
        y_block0_done = sem("y_block0_done")
        y_squared, y_out = sem("y_squared"), sem("y_out")
        ss_y_ready, rstd_y_ready = sem("ss_y_ready"), sem("rstd_y_ready")
        x2_ready, hT_filled = sem("x2_ready"), sem("hT_filled")
        hT_hi_ready, hT_lo_ready = sem("hT_hi_ready"), sem("hT_lo_ready")
        ss_x2_ready, rstd_x2_ready = sem("ss_x2_ready"), sem("rstd_x2_ready")
        relu_ready, a_ready = sem("relu_ready"), sem("a_ready")
        aT_filled, aT_hi_ready, aT_lo_ready = sem("aT_filled"), sem("aT_hi_ready"), sem("aT_lo_ready")
        acc_added = sem("acc_added")
        m_gained_pool = sem("m_gained_pool")
        m_squared, m_gained = sem("m_squared"), sem("m_gained")
        ss_m_ready, rstd_m_ready = sem("ss_m_ready"), sem("rstd_m_ready")
        m_block0_done, last_added, last_gained = sem("m_block0_done"), sem("last_added"), sem("last_gained")
        scaled_ready = sem("scaled_ready")
        y_scaled, x2_pool_ready = sem("y_scaled"), sem("x2_pool_ready")
        result_dve, result_pool = sem("result_dve"), sem("result_pool")
        dve_own, pool_own = sem("dve_own"), sem("pool_own")

        w_in, w_uq, w_ukv, w_o, w_up, w_down = (t[n][0] for n in ("w_in", "w_uq", "w_ukv", "w_o", "w_up", "w_down"))
        x_dram = t["x"][0].rearrange("(b p) d -> p b d", p=P)
        out_dram = out[0].rearrange("(b p) d -> p b d", p=P)

        def rows(w, k0, nk, cols):
            return w[k0 * P:(k0 + nk) * P, cols].rearrange("(c p) n -> p c n", p=P)

        def quad_source(n):
            z = quads[n]
            if z["kind"] == "in":
                return rows(w_in, 4 * z["q"], 4, slice(z["col"], z["col"] + z["width"]))
            if z["kind"] == "kv":
                return rows(w_ukv, 0, 4, slice(z["p"] * W, (z["p"] + 1) * W))
            if z["kind"] == "q":
                return rows(w_uq, 3 * z["part"], 3, slice(z["p"] * QW, (z["p"] + 1) * QW))
            if z["kind"] == "out":
                return rows(w_o, 4 * z["q"], 4, slice(z["col"], z["col"] + W))
            if z["kind"] == "up":
                return rows(w_up, 4 * z["q"], 4, slice(z["j"] * W, (z["j"] + 1) * W))
            return rows(w_down, 4 * z["j"], 4, slice(z["q"] * W, (z["q"] + 1) * W))

        def half_shape(h):
            if h // 2 not in quads:
                return (h % 2) * 2 * W, 2 * W
            z = quads[h // 2]
            first = 2 * z["width"] * (h % 2)
            return first, z["width"] * min(2, z["nk"] - 2 * (h % 2))

        def chunk_of(n, k, width):
            slot = (2 * n + k // 2) % AHEAD
            cols = slice((k % 2) * width, (k % 2 + 1) * width)
            return w_hi[:, slot, cols], w_lo[:, slot, cols]

        def blocks(tile, k, tb):
            return tile[:, k, tb * P:(tb + 1) * P]

        def f32(ap):
            return ap.bitcast(F32)

        X_BANK = [2 + j % 6 for j in range(8)]
        LAT_BANK = [4, 5, 7, 4, 5]
        LAT_CHUNK = [("kv", 0), ("kv", 2), ("q", 0), ("q", 2), ("q", 4)]

        def lat_cols(j, c):
            kind, k = LAT_CHUNK[j]
            return (0 if kind == "q" else Q_RANK) + (k + c) * P

        def latT_dst(j, c):
            kind, k = LAT_CHUNK[j]
            if kind == "q":
                return cqT_hi[:, k + c, :], cqT_lo[:, k + c, :], G_Q + k + c
            return yT_hi[:, KV_AT + k + c, :], yT_lo[:, KV_AT + k + c, :], G_KV + k + c

        DVE_PARTS = 3

        def m_add_index(what, q):
            return 2 * int(what[-1]) + q - 2

        X2_DVE = 4

        def x2_block_part(a):
            return a // 2, a % 2

        def hT_parts(a):
            if a < X2_DVE:
                tb, q = x2_block_part(a)
                return [(4 * q + c, slice(tb * P, (tb + 1) * P), slice(c * P, (c + 1) * P)) for c in range(4)]
            return [(2 * a + c, slice(0, SEQ), slice(c * SEQ, (c + 1) * SEQ)) for c in range(2)]

        RESIDUAL_QUAD = min(n for n, z in quads.items() if z["kind"] == "out") + 2

        def up_bank(j):
            return 6 if j == 1 else 0

        def conv_bank(half, c):
            return 7 if half == 0 else 4 + c

        def wait_kv_buffers(eng, p):
            if p >= 1:
                eng.wait_ge(kT_filled, p)
            if p >= 2:
                eng.wait_ge(pv_done, p - 1)

        block = ctx.enter_context(nc.Block())

        @block.sync
        def _(sp):
            def load_quad(slot, source, nk=4, width=W):
                dst = raw[:, slot, 0:nk * width].rearrange("p (c n) -> p c n", c=nk)
                sp.dma_start(dst, source).then_inc(raw_landed[slot], 16)

            def load_half(half, landed):
                dst = raw[:, 0, half * 2 * W:(half + 1) * 2 * W].rearrange("p (c n) -> p c n", c=2)
                sp.dma_start(dst, quad_source(0)[:, 2 * half:2 * half + 2]).then_inc(landed, 16)

            def load_x(part):
                cols = slice(*X_PARTS[part])
                sp.dma_start(x_in[:, :, cols], x_dram[:, :, cols]).then_inc(x_landed[part], 16)

            load_half(0, first_half_landed)
            sp.dma_start(ident[:], t["ident"]).then_inc(ident_landed, 16)
            sp.dma_start(gains[:], t["gains"]).then_inc(gains_landed, 16)
            load_x(0)
            load_x(1)
            load_half(1, raw_landed[0])
            for q in range(1, RAW):
                load_x(q + 1)
                load_quad(q, quad_source(q))
            sp.dma_start(cos_t[:], t["cos"]).then_inc(tables_landed, 16)
            sp.dma_start(sin_t[:], t["sin"]).then_inc(tables_landed, 16)
            for n in range(RAW, NQ):
                z = quads[n]
                sp.wait_ge(lo_ready, 2 * (n - RAW) + 2)
                load_quad(n % RAW, quad_source(n), z["nk"], z["width"])
                if n == RESIDUAL_QUAD:
                    sp.wait_ge(oT_lo_ready, PAIRS)
                    sp.dma_start(g_post_mix[:], t["post_mix_g"].to_broadcast([P, D])).then_inc(g_mix_landed, 16)
                    sp.dma_start(x_res[:], x_dram).then_inc(x_res_landed, 16)
            with sp.Fori(LOOP.start, LOOP.stop) as j:
                for i in range(8):
                    sp.wait_ge(lo_ready, (j - LOOP.start) * 16 + 2 * (NQ + i - RAW) + 2)
                    if i < 4:
                        src = rows(w_up, 4 * i, 4, bass.ds(j * W, W))
                    else:
                        src = w_down[bass.ds((j - 1) * W, W), (i - 4) * W:(i - 3) * W].rearrange(
                            "(c p) n -> p c n", p=P)
                    load_quad(i % RAW, src)
            for n in range(NQ_TAIL, NQ_ALL):
                sp.wait_ge(lo_ready, 2 * (n - RAW) + 2)
                load_quad(n % RAW, quad_source(n))
            sp.dma_start(g_post_mlp[:], t["post_mlp_g"].to_broadcast([P, D])).then_inc(g_mlp_landed, 16)
            for tb in range(TB):
                for q in range(4):
                    if q < DVE_PARTS:
                        sp.wait_ge(result_dve, DVE_PARTS * tb + q + 1)
                    else:
                        sp.wait_ge(result_pool, tb + 1)
                    cols = slice(q * W, (q + 1) * W)
                    sp.dma_start(out_dram[:, tb, cols], x_res[:, tb, cols]).then_inc(out_landed, 16)
            sp.wait_ge(out_landed, 16 * 4 * TB)

        @block.tensor
        def _(pe):
            def product(bank, width, lhs, k, wk, first, last, tbs=range(TB)):
                hi, lo = wk
                for tb in tbs:
                    dst = ps[:, bank + tb, 0:width]
                    x_hi, x_lo = blocks(lhs[0], k, tb), blocks(lhs[1], k, tb)
                    nc.tensor.matmul(dst, x_hi, hi, start=first, stop=False)
                    nc.tensor.matmul(dst, x_lo, hi, start=False, stop=False)
                    mm = nc.tensor.matmul(dst, x_hi, lo, start=False, stop=last)
                return mm

            def transposes(bank, sources):
                for i, src in enumerate(sources):
                    mm = nc.tensor.transpose(ps[:, bank, i * P:(i + 1) * P], src, ident[:])
                return mm

            def strip_bank(strip):
                return 2 * (strip % 2)

            def wait_strip_bank(strip):
                s = strip - 2
                if s < 0:
                    return
                if s < S_OUT:
                    by_act = [1, 2, 3, 4, 0, 5, 6, 0, 7][s]
                    if by_act:
                        pe.wait_ge(strip_out_act, by_act)
                    else:
                        pe.wait_ge(strip_out_dve, 1 if s < 6 else 2)
                else:
                    pe.wait_ge(y_squared, 2 * (s - S_OUT) + 2)
                    pe.wait_ge(y_out, 2 * (s - S_OUT) + 2)

            def stream(n, k, tbs=range(TB)):
                z = quads[n]
                blocks_left = TB - 1 - tbs[-1]
                width, kind = z["width"], z["kind"]
                if k % 2 == 0:
                    pe.wait_ge(lo_ready, 2 * n + k // 2 + 1)
                wk = chunk_of(n, k, width)
                if kind == "in":
                    if z["first"] and k == 0:
                        wait_strip_bank(z["strip"])
                    if z["strip"] == 0 and k % 2 == 0:
                        pe.wait_ge(xT_lo_ready, 2 * z["q"] + k // 2 + 1)
                    first, last = z["first"] and k == 0, z["last"] and k == 3
                    mm = product(strip_bank(z["strip"]), width, (xT_hi, xT_lo), 4 * z["q"] + k, wk, first, last)
                elif kind == "out":
                    if z["first"] and k == 0:
                        wait_strip_bank(z["strip"])
                        if z["strip"] == S_OUT:
                            pe.wait_ge(oT_lo_ready, PAIRS)
                    if z["strip"] == S_OUT and z["q"] < 2 and k == 0:
                        pe.wait_ge(convT_ready, 4 * z["q"] + 4)
                    first, last = z["first"] and k == 0, z["last"] and k == 3
                    mm = product(strip_bank(z["strip"]), width, (yT_hi, yT_lo), 4 * z["q"] + k, wk, first, last,
                                 tbs)
                    if last and blocks_left:
                        mm.then_inc(y_block0_done, 1)
                elif kind == "kv":
                    if k == 0:
                        if z["p"] == 0:
                            pe.wait_ge(latT_lo_ready, 5)
                        else:
                            pe.wait_ge(probs_ready, 2 * z["p"])
                            pe.wait_ge(probsT0_ready, z["p"])
                    last = k == 3
                    mm = product(4, width, (yT_hi, yT_lo), KV_AT + k, wk, k == 0, last)
                elif kind == "q":
                    if k == 0 and z["part"] == 0:
                        pe.wait_ge(kv0_ready, z["p"] + 1)
                        pe.wait_ge(kv1_ready, z["p"] + 1)
                    last = z["part"] == 1 and k == 2
                    mm = product(4, width, (cqT_hi, cqT_lo), 3 * z["part"] + k, wk,
                                 z["part"] == 0 and k == 0, last)
                elif kind == "up":
                    if k == 0:
                        if z["j"] == 0 and len(tbs) == 1:
                            pe.wait_ge(hT_lo_ready, 2 * tbs[0] + z["q"] + 1)
                            pe.wait_ge(y_squared, 7 + tbs[0])
                            pe.wait_ge(y_out, 7 + tbs[0])
                        elif z["j"] == 0:
                            pe.wait_ge(hT_lo_ready, 2 * z["q"] + 2)
                        elif z["j"] > 1 and z["q"] == 0:
                            pe.wait_ge(relu_ready, z["j"])
                    mm = product(up_bank(z["j"]), width, (xT_hi, xT_lo), 4 * z["q"] + k, wk,
                                 z["q"] == 0 and k == 0, z["q"] == 3 and k == 3, tbs)
                else:
                    if k == 0:
                        pe.wait_ge(aT_lo_ready, z["j"] + 1)
                        pe.wait_ge(acc_added, 4 * z["j"] + z["q"] + 1)
                        if z["j"] == 0:
                            pe.wait_ge(relu_ready, 1 + (z["q"] > 0))
                    at = 4 if z["j"] == FF_STRIPS - 1 else 0
                    mm = product(4 + 2 * (z["q"] % 2), width, (yT_hi, yT_lo), at + k, wk, k == 0, k == 3, tbs)
                    if k == 3 and blocks_left:
                        mm.then_inc(m_block0_done, 1)
                if not blocks_left and (k % 2 == 1 or k == z["nk"] - 1):
                    mm.then_inc(half_used, 1)

            pe.wait_ge(ones_ready, 1)
            for _ in range(WARM_UP):
                nc.tensor.matmul(ps[:, 0, 0:P], ones[:], ones[:], start=True, stop=True)
            pe.wait_ge(ident_landed, 16)

            def hidden_transposes(j, used=True):
                pe.wait_ge(a_ready, j + 1)
                if used:
                    pe.wait_ge(aT_lo_ready, j)
                for tb in range(TB):
                    mm = transposes(2 + tb, [a_sb[:, tb, c * P:(c + 1) * P] for c in range(4)])
                mm.then_inc(aT_filled, 1)

            def down_quad(i, half, added):
                pe.wait_ge(acc_added, added)
                for k in range(4):
                    if k % 2 == 0:
                        pe.wait_ge(lo_ready, half + k // 2 + 1)
                    mm = product(4 + 2 * (i % 2), W, (yT_hi, yT_lo), k, chunk_of(i, k, W), k == 0, k == 3)
                    if k % 2:
                        mm.then_inc(half_used, 1)

            def step(what, a, b):
                if what == "mm":
                    stream(a, b)
                elif what == "mm_b0":
                    stream(a, b, [0])
                elif what == "mm_b1":
                    stream(a, b, [1])
                elif what == "xT":
                    pe.wait_ge(x_landed[a if a < 2 else 1 + a // 2], 16)
                    if a >= 6:
                        pe.wait_ge(xT_lo_ready, a - 5)
                    transposes(X_BANK[a], [x_in[:, tb, (2 * a + c) * P:(2 * a + c + 1) * P]
                                           for c in range(2) for tb in range(TB)]).then_inc(xT_filled, 1)
                elif what == "latT":
                    pe.wait_ge(lat_ready, 1)
                    if a >= 3:
                        pe.wait_ge(latT_lo_ready, a - 2)
                    transposes(LAT_BANK[a], [lat[:, tb, lat_cols(a, c):lat_cols(a, c) + P]
                                             for c in range(2) for tb in range(TB)]).then_inc(latT_filled, 1)
                elif what == "krT":
                    pe.wait_ge(kr_ready, 4)
                    transposes(6, [kr_rot[:, tb].rearrange("p e r -> p (e r)")
                                   for tb in range(TB)]).then_inc(krT_filled, 1)
                elif what == "kT":
                    pe.wait_ge(q_ready, a + 1)
                    pe.wait_ge(kv0_ready, a + 1)
                    pe.wait_ge(kv1_ready, a + 1)
                    transposes(4, [k_sb[:, tb, h] for h in range(2) for tb in range(TB)]).then_inc(kT_filled, 1)
                elif what == "qT":
                    pe.wait_ge(q_ready, a + 1)
                    transposes(5, [q_sb[:, tb, h * (NOPE + ROPE):h * (NOPE + ROPE) + NOPE]
                                   for h in range(2) for tb in range(TB)]).then_inc(qT_filled, 1)
                elif what == "qrT":
                    pe.wait_ge(q_rope_ready, 4 * (a + 1))
                    pe.wait_ge(kT_ready, a + 1)
                    transposes(4, [qr_rot[:, tb].rearrange("p e r -> p (e r)")
                                   for tb in range(TB)]).then_inc(qrT_filled, 1)
                elif what == "scores":
                    p, h = a, b
                    pe.wait_ge(kT_ready, p + 1)
                    pe.wait_ge(qT_ready, p + 1)
                    pe.wait_ge(qrT_ready, p + 1)
                    pe.wait_ge(krT_ready, 1)
                    if p and not h:
                        pe.wait_ge(oT_lo_ready, p)
                    bank, rp = (6, 4)[h], slice(ROPE * h, ROPE * (h + 1))
                    for tb, cols, keys in [(0, slice(0, P), slice(0, P)), (1, slice(P, 3 * P), slice(0, SEQ))]:
                        nc.tensor.matmul(ps[:, bank, cols], qT_sb[:, h, tb * P:(tb + 1) * P], kT_sb[:, h, keys],
                                         start=True, stop=False)
                        mm = nc.tensor.matmul(ps[:, bank, cols], qrT_sb[rp, tb * P:(tb + 1) * P], krT[rp, keys],
                                              start=False, stop=True)
                    mm.then_inc(scores_done, 1)
                elif what == "probsT":
                    pe.wait_ge(probs_ready, 2 * a + b + 1)
                    if b == 0:
                        pe.wait_ge(qT_ready, a + 1)
                    transposes((5, 6)[b], [probs[:, b, i * P:(i + 1) * P] for i in range(3)]
                               ).then_inc(probsT_filled, 1)
                elif what == "pv":
                    pe.wait_ge(kv0_ready, a + 1)
                    pe.wait_ge(kv1_ready, a + 1)
                    pe.wait_ge(probsT0_ready, a + 1)
                    pe.wait_ge(probsT1_ready, a + 1)
                    for h in range(2):
                        o = [ps[:, 6, (2 * h + tb) * P:(2 * h + tb + 1) * P] for tb in range(TB)]
                        v = [v_sb[:, a % 2, tb, h] for tb in range(TB)]
                        nc.tensor.matmul(o[0], probsT[:, h, 0:P], v[0], start=True, stop=True)
                        nc.tensor.matmul(o[1], probsT[:, h, P:2 * P], v[0], start=True, stop=False)
                        mm = nc.tensor.matmul(o[1], probsT[:, h, 2 * P:3 * P], v[1], start=False, stop=True)
                    mm.then_inc(pv_done, 1)
                elif what == "oT":
                    pe.wait_ge(o_normed, a + 1)
                    transposes(6, [o_sb[:, h, tb] for h in range(2) for tb in range(TB)]).then_inc(oT_filled, 1)
                elif what == "convT":
                    pe.wait_ge(strip_out_dve, a + 1)
                    pe.wait_ge(strip_out_act, (5, 7)[a])
                    if a:
                        pe.wait_ge(oT_lo_ready, PAIRS)
                        if conv_bank(a, b) == conv_bank(0, 0):
                            pe.wait_ge(conv_std_ready, 4)
                    elif b:
                        pe.wait_ge(conv_std_ready, b)
                    else:
                        pe.wait_ge(latT_lo_ready, 3)
                    transposes(conv_bank(a, b), [s[:, a, tb, b * P:(b + 1) * P] for s in (u_sb, b_sb)
                                                 for tb in range(TB)]).then_inc(convT_filled, 1)
                elif what == "conv_norm":
                    i = 4 * a + b
                    pe.wait_ge(ones_ready, 1)
                    pe.wait_ge(conv_sq_ready, i + 1)
                    nc.tensor.matmul(ps[:, conv_bank(a, b), 0:SEQ], ones[:], conv_s[:, i % NCONV, :],
                                     start=True, stop=True).then_inc(conv_sum_done, 1)
                elif what == "hT":
                    if a < X2_DVE:
                        pe.wait_ge(x2_ready, a + 1)
                    else:
                        pe.wait_ge(x2_pool_ready, a - X2_DVE + 1)
                    if a >= 4:
                        pe.wait_ge(hT_lo_ready, a - 3)
                    transposes(4 + a % 4, [x_res[:, t0 // P, k * P:(k + 1) * P]
                                           for k, tokens, _ in hT_parts(a)
                                           for t0 in range(tokens.start, tokens.stop, P)]).then_inc(hT_filled, 1)
                elif what == "aT":
                    hidden_transposes(a, used=a > 0)

            for what, a, b in steps:
                step(what, a, b)
            with pe.Fori(LOOP.start, LOOP.stop) as j:
                base = (j - LOOP.start) * 16 + 2 * NQ
                pe.wait_ge(relu_ready, j)
                for i in range(4):
                    for k in range(4):
                        if k % 2 == 0:
                            pe.wait_ge(lo_ready, base + (2 * i + k // 2 + 1))
                        mm = product(0, W, (xT_hi, xT_lo), 4 * i + k, chunk_of(i, k, W),
                                     i == 0 and k == 0, i == 3 and k == 3)
                        if k % 2:
                            mm.then_inc(half_used, 1)
                pe.wait_ge(aT_lo_ready, j)
                for i in range(4):
                    down_quad(i, base + (8 + 2 * i), (j - 1) * 4 + (i + 1))
                hidden_transposes(j)
            for what, a, b in tail:
                step(what, a, b)

        @block.scalar
        def _(act):
            def split_hi(slot, raw_slot, first, size, used, landed_sem, landed):
                if used is not None:
                    act.wait_ge(half_used, used)
                act.wait_ge(landed_sem, landed)
                nc.scalar.activation(w_hi[:, slot, 0:size], raw[:, raw_slot, first:first + size],
                                     ACT.Copy).then_inc(hi_ready, 1)

            def split_static(h):
                n = h // 2
                if n >= NQ_ALL:
                    return
                first, size = half_shape(h)
                split_hi(h % AHEAD, n % RAW, first, size, h - AHEAD + 1 if h >= AHEAD else None,
                         raw_landed[n % RAW] if h else first_half_landed, 16 * (n // RAW + 1))

            def scaled_out(dst, bank, width, scale):
                for tb in range(TB):
                    ins = nc.scalar.activation(dst[tb], ps[:, bank + tb, 0:width], ACT.Copy,
                                               scale=scale[:, tb:tb + 1])
                return ins

            def gained_hi(dst, bank, gain):
                for c in range(2):
                    ins = nc.scalar.activation(dst[c], ps[:, bank, c * SEQ:(c + 1) * SEQ], ACT.Copy,
                                               scale=gains[:, gain[c]:gain[c] + 1])
                return ins

            def relu_out(j, done, bank=0):
                act.wait_ge(half_used, done)
                for tb in range(TB):
                    ins = nc.scalar.activation(a_sb[:, tb], ps[:, bank + tb], ACT.Relu, scale=rstd_x2[:, tb:tb + 1])
                ins.then_inc(relu_ready, 1)

            def hidden_hi(j, at=0):
                act.wait_ge(aT_filled, j + 1)
                for tb in range(TB):
                    ins = nc.scalar.activation(yT_hi[:, at:at + 4, tb * P:(tb + 1) * P],
                                               ps[:, 2 + tb].rearrange("p (c t) -> p c t", c=4), ACT.Copy)
                ins.then_inc(aT_hi_ready, 1)

            act.wait_ge(ones_ready, 1)
            nc.scalar.activation(rstd_m[:], ones[:, 0:TB], ACT.Copy)
            def step(what, a, b):
                if what in ("mm", "mm_b1"):
                    if b % 2 == 1 or b == quads[a]["nk"] - 1:
                        split_static(2 * a + b // 2 + AHEAD)
                elif what == "split":
                    split_static(a)
                elif what == "xT":
                    act.wait_ge(xT_filled, a + 1)
                    act.wait_ge(gains_landed, 16)
                    gained_hi([xT_hi[:, 2 * a + c] for c in range(2)], X_BANK[a],
                              [G_MIX + 2 * a + c for c in range(2)]).then_inc(xT_hi_ready, 1)
                elif what == "x_stats":
                    for landed in x_landed:
                        act.wait_ge(landed, 16)
                    for tb in range(TB):
                        if tb:
                            act.wait_ge(ss_x_ready, tb)
                        nc.scalar.activation(lat.rearrange("p b n -> p (b n)")[:, 0:D], x_in[:, tb], ACT.Square,
                                             accum_out=ss_x[:, tb:tb + 1]).then_inc(ss_x_ready, 1)
                elif what == "lat_out":
                    act.wait_ge(half_used, 2 * b + 2)
                    act.wait_ge(rstd_x_ready, 1)
                    if a == 0:
                        act.wait_ge(ss_x_ready, 2)
                    width = quads[b]["width"]
                    scaled_out([lat[:, tb, a * W:a * W + width] for tb in range(TB)], 2 * (a % 2), width,
                               rstd_x).then_inc(strip_out_act, 1)
                elif what == "lat_norm":
                    act.wait_ge(strip_out_act, 3)
                    for i, (c0, c1) in enumerate([(0, Q_RANK), (Q_RANK, Q_RANK + KV_RANK)]):
                        for tb in range(TB):
                            if i or tb:
                                act.wait_ge(ss_lat_ready, 2 * i + tb)
                            nc.scalar.activation(u_sb[:, 0].rearrange("p b n -> p (b n)")[:, 0:c1 - c0],
                                                 lat[:, tb, c0:c1], ACT.Square,
                                                 accum_out=ss_lat[:, 2 * i + tb:2 * i + tb + 1]
                                                 ).then_inc(ss_lat_ready, 1)
                elif what == "latT":
                    act.wait_ge(latT_filled, a + 1)
                    dst = [latT_dst(a, c) for c in range(2)]
                    gained_hi([d[0] for d in dst], LAT_BANK[a], [d[2] for d in dst]).then_inc(latT_hi_ready, 1)
                elif what == "kv_out":
                    act.wait_ge(half_used, 2 * b + 2)
                    wait_kv_buffers(act, a)
                    kv = ps[:, 4].rearrange("p (h e n) -> p h e n", h=2, e=2)
                    nc.scalar.activation(k_sb[:, 0], kv[:, :, 0], ACT.Copy)
                    nc.scalar.activation(v_sb[:, a % 2, 0], kv[:, :, 1], ACT.Copy).then_inc(kv0_ready, 1)
                elif what == "q_out":
                    act.wait_ge(half_used, 2 * b + 2)
                    if a:
                        act.wait_ge(q_rope_ready, 4 * a)
                        act.wait_ge(qT_filled, a)
                    for tb in range(TB):
                        ins = nc.scalar.activation(q_sb[:, tb], ps[:, 4 + tb, 0:QW], ACT.Copy)
                    ins.then_inc(q_ready, 1)
                elif what == "qT":
                    act.wait_ge(qT_filled, a + 1)
                    if a:
                        act.wait_ge(scores_done, 2 * a)
                    nc.scalar.activation(qT_sb.rearrange("p h t -> p (h t)"), ps[:, 5],
                                         ACT.Copy).then_inc(qT_ready, 1)
                elif what == "scores":
                    i = 2 * a + b
                    act.wait_ge(neg_max_ready, i + 1)
                    if a:
                        act.wait_ge(probsT_filled, i - 1)
                    bank = (6, 4)[b]
                    for tb, cols in [(0, slice(0, P)), (1, slice(P, 3 * P))]:
                        s = 2 * b + tb
                        ins = nc.scalar.activation(probs[:, b, cols], ps[:, bank, cols], ACT.Exp, scale=SCALE,
                                                   bias=neg_max[:, s:s + 1], accum_out=row_sum[:, s:s + 1])
                    ins.then_inc(probs_ready, 1)
                elif what == "probsT" and b == 1:
                    act.wait_ge(probsT_filled, 2 * a + 2)
                    if a:
                        act.wait_ge(pv_done, a)
                    nc.scalar.activation(probsT[:, 1], ps[:, 6, 0:3 * P], ACT.Copy).then_inc(probsT1_ready, 1)
                elif what == "oT":
                    act.wait_ge(oT_filled, a + 1)
                    gained_hi([yT_hi[:, 8 + 2 * a + h] for h in range(2)], 6,
                              [G_ATT + 2 * a + h for h in range(2)]).then_inc(oT_hi_ready, 1)
                elif what == "conv_out" and CONV_PARTS[a] != "c":
                    act.wait_ge(half_used, 2 * b + 2)
                    if a == 0:
                        act.wait_ge(ss_lat_ready, 4)
                    dst = u_sb if CONV_PARTS[a] == "u" else b_sb
                    scaled_out([dst[:, a // 3, tb] for tb in range(TB)], 2 * ((S_CONV + a) % 2), W,
                               rstd_x).then_inc(strip_out_act, 1)
                elif what == "convT":
                    i = 4 * a + b
                    act.wait_ge(convT_filled, i + 1)
                    if i >= NCONV:
                        act.wait_ge(convT_ready, i - NCONV + 1)
                    tap = G_TAP + 2 * 8 + i
                    nc.scalar.activation(conv_y[:, i % NCONV], ps[:, conv_bank(a, b), 0:SEQ], ACT.Copy,
                                         scale=gains[:, tap:tap + 1]).then_inc(tap_ready, 1)
                elif what == "conv_square":
                    i = 4 * a + b
                    act.wait_ge(conv_y_ready, i + 1)
                    nc.scalar.activation(conv_s[:, i % NCONV], conv_y[:, i % NCONV],
                                         ACT.Square).then_inc(conv_sq_ready, 1)
                elif what == "conv_norm":
                    i = 4 * a + b
                    act.wait_ge(conv_sum_done, i + 1)
                    nc.scalar.activation(conv_s[:, i % NCONV], ps[:, conv_bank(a, b), 0:SEQ], ACT.Sqrt,
                                         scale=1.0 / P, bias=eps_col[:, 0:1]).then_inc(conv_std_ready, 1)
                elif what == "y_out":
                    act.wait_ge(half_used, 2 * b + 2)
                    if a:
                        act.wait_ge(y_squared, 2 * a)
                    for tb in range(TB):
                        if tb:
                            act.wait_ge(y_out, 2 * a + 1)
                        nc.scalar.activation(a_sb[:, tb], ps[:, 2 * ((S_OUT + a) % 2) + tb], ACT.Square,
                                             accum_out=ss_strip[:, tb, a:a + 1]).then_inc(y_squared, 1)
                elif what == "y_block":
                    if a == 0:
                        act.wait_ge(y_block0_done, 1)
                        act.wait_ge(y_squared, 6)
                    else:
                        act.wait_ge(half_used, 2 * b + 2)
                    nc.scalar.activation(a_sb[:, a], ps[:, 2 * ((S_OUT + 3) % 2) + a], ACT.Square,
                                         accum_out=ss_strip[:, a, 3:4]).then_inc(y_squared, 1)
                elif what == "h_split":
                    act.wait_ge(hT_filled, a + 1)
                    for k, tokens, cols in hT_parts(a):
                        ins = nc.scalar.activation(xT_hi[:, k, tokens], ps[:, 4 + a % 4, cols], ACT.Copy,
                                                   scale=gains[:, G_MLP + k:G_MLP + k + 1])
                    ins.then_inc(hT_hi_ready, 1)
                elif what == "x2_stats":
                    act.wait_ge(x2_ready, X2_DVE)
                    act.wait_ge(x2_pool_ready, 8 - X2_DVE)
                    for tb in range(TB):
                        nc.scalar.activation(acc[:, tb], x_res[:, tb], ACT.Square,
                                             accum_out=ss_x[:, tb:tb + 1]).then_inc(ss_x2_ready, 1)
                elif what == "relu":
                    act.wait_ge(rstd_x2_ready, 1)
                    if a:
                        act.wait_ge(aT_filled, a)
                    relu_out(a, 2 * b + 2, up_bank(a))
                elif what == "aT":
                    hidden_hi(a, b)
                elif what == "m_square":
                    act.wait_ge(acc_added, 4 * FF_STRIPS + a - 1)
                    if a:
                        act.wait_ge(m_squared, a)
                    for tb in range(TB):
                        ins = nc.scalar.activation(a_sb[:, tb], acc[:, tb, a * W:(a + 1) * W], ACT.Square,
                                                   accum_out=ss_strip[:, tb, a:a + 1])
                    ins.then_inc(m_squared, 1)
                elif what.startswith("m_add"):
                    tb, i = int(what[-1]), m_add_index(what, a)
                    act.wait_ge(last_added, i + 1)
                    act.wait_ge(m_squared, 2 + i)
                    nc.scalar.activation(a_sb[:, tb], acc[:, tb, a * W:(a + 1) * W], ACT.Square,
                                         accum_out=ss_strip[:, tb, a:a + 1]).then_inc(m_squared, 1)
                    if a == 3:
                        act.wait_ge(rstd_m_ready, tb + 1)
                        act.wait_ge(last_gained, tb + 1)
                        act.wait_ge(m_squared, 2 + i + 1)
                        nc.scalar.activation(a_sb[:, tb], gained[:, tb], ACT.Copy,
                                             scale=rstd_m[:, tb:tb + 1]).then_inc(scaled_ready, 1)

            for what, a, b in steps:
                step(what, a, b)
            with act.Fori(LOOP.start, LOOP.stop) as j:
                base = (j - LOOP.start) * 16 + 2 * NQ
                for i in range(16):
                    if i == 7:
                        relu_out(j, base + 8)
                    slot = (i + AHEAD) // 2 % RAW
                    split_hi(i % AHEAD, slot, (i % 2) * 2 * W, 2 * W, base + (i + 1), raw_landed[slot],
                             (j - LOOP.start) * 32 + 16 * ((2 * NQ + i + AHEAD) // (2 * RAW) + 1))
                hidden_hi(j)
            for what, a, b in tail:
                step(what, a, b)

        @block.vector
        def _(dve):
            def own(ins):
                own.count += 1
                ins.then_inc(dve_own, 1)
                dve.wait_ge(dve_own, own.count)
            own.count = 0

            def split_lo(slot, raw_slot, first, size, ready):
                dve.wait_ge(hi_ready, ready)
                nc.vector.tensor_tensor(w_lo[:, slot, 0:size], raw[:, raw_slot, first:first + size],
                                        f32(w_hi[:, slot, 0:size]), ALU.subtract).then_inc(lo_ready, 1)

            def split_static(h):
                if h // 2 >= NQ_ALL:
                    return
                first, size = half_shape(h)
                split_lo(h % AHEAD, h // 2 % RAW, first, size, h + 1)

            def gained_lo(hi, lo, bank, gain):
                for c in range(2):
                    ins = nc.vector.scalar_tensor_tensor(
                        out=lo[c], in0=ps[:, bank, c * SEQ:(c + 1) * SEQ], scalar=gains[:, gain[c]:gain[c] + 1],
                        in1=f32(hi[c]), op0=ALU.mult, op1=ALU.subtract)
                return ins

            def hidden_lo(j, at=0):
                dve.wait_ge(aT_hi_ready, j + 1)
                for tb in range(TB):
                    dst = (slice(None), slice(at, at + 4), slice(tb * P, (tb + 1) * P))
                    ins = nc.vector.tensor_tensor(yT_lo[dst], ps[:, 2 + tb].rearrange("p (c t) -> p c t", c=4),
                                                  f32(yT_hi[dst]), ALU.subtract)
                ins.then_inc(aT_lo_ready, 1)

            def add_down(i, done, added):
                dve.wait_ge(half_used, done)
                dve.wait_ge(acc_added, added)
                m = acc[:, :, i * W:(i + 1) * W]
                bank = 4 + 2 * (i % 2)
                nc.vector.tensor_tensor(m, m, ps[:, bank:bank + 2], ALU.add).then_inc(acc_added, 1)

            def finish(tb, q):
                dve.wait_ge(rstd_m_ready, tb + 1)
                if q < 2:
                    dve.wait_ge(m_gained_pool, 2 * q + 2)
                else:
                    dve.wait_ge(m_gained, tb + 1)
                cols = slice(q * W, (q + 1) * W)
                nc.vector.scalar_tensor_tensor(
                    out=x_res[:, tb, cols], in0=acc[:, tb, cols], scalar=rstd_m[:, tb:tb + 1],
                    in1=x_res[:, tb, cols], op0=ALU.mult, op1=ALU.add).then_inc(result_dve, 1)


            def step(what, a, b):
                if what in ("mm", "mm_b1"):
                    if b % 2 == 1 or b == quads[a]["nk"] - 1:
                        split_static(2 * a + b // 2 + AHEAD)
                elif what == "split":
                    split_static(a)
                elif what == "xT":
                    dve.wait_ge(xT_hi_ready, a + 1)
                    dve.wait_ge(gains_landed, 16)
                    ks = [2 * a, 2 * a + 1]
                    gained_lo([xT_hi[:, k] for k in ks], [xT_lo[:, k] for k in ks], X_BANK[a],
                              [G_MIX + k for k in ks]).then_inc(xT_lo_ready, 1)
                elif what == "lat_norm":
                    dve.wait_ge(rstd_lat_ready, 1)
                    dve.wait_ge(strip_out_act, 3)
                    for i, (c0, c1) in enumerate([(0, Q_RANK), (Q_RANK, Q_RANK + KV_RANK)]):
                        for tb in range(TB):
                            ins = nc.vector.tensor_scalar(lat[:, tb, c0:c1], lat[:, tb, c0:c1],
                                                          rstd_lat[:, 2 * i + tb:2 * i + tb + 1], None, ALU.mult)
                    ins.then_inc(lat_ready, 1)
                elif what == "latT":
                    dve.wait_ge(latT_hi_ready, a + 1)
                    dst = [latT_dst(a, c) for c in range(2)]
                    gained_lo([d[0] for d in dst], [d[1] for d in dst], LAT_BANK[a],
                              [d[2] for d in dst]).then_inc(latT_lo_ready, 1)
                elif what == "krT":
                    dve.wait_ge(krT_filled, 1)
                    nc.vector.tensor_copy(krT[:], ps[:, 6, 0:SEQ]).then_inc(krT_ready, 1)
                elif what == "kv_out":
                    dve.wait_ge(half_used, 2 * b + 2)
                    wait_kv_buffers(dve, a)
                    kv = ps[:, 5].rearrange("p (h e n) -> p h e n", h=2, e=2)
                    nc.vector.tensor_copy(k_sb[:, 1], kv[:, :, 0])
                    nc.vector.tensor_copy(v_sb[:, a % 2, 1], kv[:, :, 1]).then_inc(kv1_ready, 1)
                elif what == "kT":
                    dve.wait_ge(kT_filled, a + 1)
                    if a:
                        dve.wait_ge(scores_done, 2 * a)
                    nc.vector.tensor_copy(kT_sb.rearrange("p h t -> p (h t)"), ps[:, 4]).then_inc(kT_ready, 1)
                elif what == "qrT":
                    dve.wait_ge(qrT_filled, a + 1)
                    nc.vector.tensor_copy(qrT_sb[:], ps[:, 4, 0:SEQ]).then_inc(qrT_ready, 1)
                elif what == "scores":
                    i, bank = 2 * a + b, (6, 4)[b]
                    dve.wait_ge(scores_done, i + 1)
                    if a:
                        dve.wait_ge(probs_ready, i - 1)
                    nc.vector.memset(ps[0:CHUNK, bank, CHUNK:P], MASKED)
                    own(nc.vector.memset(ps[0:CHUNK, bank, 2 * P + CHUNK:3 * P], MASKED))
                    s = 2 * b
                    nc.vector.reduce_max(row_max[:, s:s + 1], ps[:, bank, 0:P], AX_X)
                    own(nc.vector.reduce_max(row_max[:, s + 1:s + 2], ps[:, bank, P:3 * P], AX_X))
                    nc.vector.tensor_scalar(neg_max[:, s:s + 2], row_max[:, s:s + 2], -SCALE, None,
                                            ALU.mult).then_inc(neg_max_ready, 1)
                elif what == "probsT" and b == 0:
                    dve.wait_ge(probsT_filled, 2 * a + 1)
                    if a:
                        dve.wait_ge(pv_done, a)
                    nc.vector.tensor_copy(probsT[:, 0], ps[:, 5, 0:3 * P]).then_inc(probsT0_ready, 1)
                elif what == "pv":
                    dve.wait_ge(probs_ready, 2 * a + 2)
                    own(nc.vector.reciprocal(inv_sum[:], row_sum[:]))
                    dve.wait_ge(pv_done, a + 1)
                    if a:
                        dve.wait_ge(oT_filled, a)
                    nc.vector.tensor_tensor(o_sb.rearrange("p h b n -> p (h b) n"),
                                            ps[:, 6].rearrange("p (s n) -> p s n", n=V_DIM),
                                            inv_sum[:].unsqueeze(2).to_broadcast([P, 4, V_DIM]),
                                            ALU.mult).then_inc(o_ready, 1)
                elif what == "o_squares":
                    dve.wait_ge(o_sq_ready, a + 1)
                    nc.vector.reduce_sum(ss_o[:], o_sq.rearrange("p h b n -> p (h b) n"), AX_X
                                         ).then_inc(ss_o_ready, 1)
                elif what == "o_norm":
                    dve.wait_ge(rstd_o_ready, a + 1)
                    o = o_sb.rearrange("p h b n -> p (h b) n")
                    nc.vector.tensor_tensor(o, o, rstd_o[:].unsqueeze(2).to_broadcast([P, 4, V_DIM]),
                                            ALU.mult).then_inc(o_normed, 1)
                elif what == "oT":
                    dve.wait_ge(oT_hi_ready, a + 1)
                    ks = [8 + 2 * a, 9 + 2 * a]
                    gained_lo([yT_hi[:, k] for k in ks], [yT_lo[:, k] for k in ks], 6,
                              [G_ATT + 2 * a, G_ATT + 2 * a + 1]).then_inc(oT_lo_ready, 1)
                elif what == "conv_out" and CONV_PARTS[a] == "c":
                    dve.wait_ge(half_used, 2 * b + 2)
                    dve.wait_ge(strip_out_act, 4 if a < 3 else 6)
                    for tb in range(TB):
                        ins = nc.vector.scalar_tensor_tensor(
                            out=u_sb[:, a // 3, tb], in0=ps[:, 2 * ((S_CONV + a) % 2) + tb],
                            scalar=rstd_x[:, tb:tb + 1], in1=u_sb[:, a // 3, tb], op0=ALU.mult, op1=ALU.mult)
                    ins.then_inc(strip_out_dve, 1)
                elif what == "convT":
                    i = 4 * a + b
                    dve.wait_ge(tap_ready, i + 1)
                    y, bank = conv_y[:, i % NCONV], conv_bank(a, b)
                    for back in (1, 2):
                        tap = G_TAP + 8 * (2 - back) + i
                        own(nc.vector.scalar_tensor_tensor(
                            out=y[:, back:SEQ], in0=ps[:, bank, 0:SEQ - back], scalar=gains[:, tap:tap + 1],
                            in1=y[:, back:SEQ], op0=ALU.mult, op1=ALU.add))
                    nc.vector.tensor_tensor(y, y, ps[:, bank, SEQ:2 * SEQ], ALU.mult).then_inc(conv_y_ready, 1)
                elif what == "conv_norm":
                    i = 4 * a + b
                    y, s = conv_y[:, i % NCONV], conv_s[:, i % NCONV]
                    dve.wait_ge(conv_std_ready, i + 1)
                    own(nc.vector.reciprocal(s, s))
                    own(nc.vector.scalar_tensor_tensor(out=y, in0=y, scalar=gains[:, G_CONV + i:G_CONV + i + 1],
                                                       in1=s, op0=ALU.mult, op1=ALU.mult))
                    own(nc.vector.tensor_copy(yT_hi[:, i], y))
                    nc.vector.tensor_tensor(yT_lo[:, i], y, f32(yT_hi[:, i]), ALU.subtract
                                            ).then_inc(convT_ready, 1)
                elif what == "y_out":
                    dve.wait_ge(half_used, 2 * b + 2)
                    dve.wait_ge(g_mix_landed, 16)
                    for tb in (1, 0):
                        if tb == 0:
                            dve.wait_ge(y_squared, 2 * a + 1)
                        nc.vector.tensor_tensor(
                            acc[:, tb, a * W:(a + 1) * W], ps[:, 2 * ((S_OUT + a) % 2) + tb],
                            g_post_mix[:, a * W:(a + 1) * W], ALU.mult).then_inc(y_out, 1)
                elif what == "y_partial":
                    dve.wait_ge(y_squared, 6)
                    nc.vector.reduce_sum(ss_row[:], ss_strip[:, :, 0:3], AX_X).then_inc(ss_y_ready, 1)
                elif what == "y_last":
                    dve.wait_ge(y_squared, 7 + a)
                    nc.vector.tensor_tensor(acc[:, a, 3 * W:], ps[:, 2 * ((S_OUT + 3) % 2) + a],
                                            g_post_mix[:, 3 * W:], ALU.mult).then_inc(y_out, 1)
                elif what == "x2" and a < X2_DVE:
                    tb, q = x2_block_part(a)
                    dve.wait_ge(rstd_y_ready, tb + 1)
                    dve.wait_ge(y_out, 4)
                    dve.wait_ge(x_res_landed, 16)
                    cols = slice(q * W, (q + 1) * W)
                    nc.vector.scalar_tensor_tensor(
                        out=x_res[:, tb, cols], in0=acc[:, tb, cols], scalar=rstd_row[:, tb:tb + 1],
                        in1=x_res[:, tb, cols], op0=ALU.mult, op1=ALU.add).then_inc(x2_ready, 1)
                elif what == "h_split":
                    dve.wait_ge(hT_hi_ready, a + 1)
                    for k, tokens, cols in hT_parts(a):
                        ins = nc.vector.scalar_tensor_tensor(
                            out=xT_lo[:, k, tokens], in0=ps[:, 4 + a % 4, cols],
                            scalar=gains[:, G_MLP + k:G_MLP + k + 1], in1=f32(xT_hi[:, k, tokens]),
                            op0=ALU.mult, op1=ALU.subtract)
                    ins.then_inc(hT_lo_ready, 1)
                elif what == "aT":
                    hidden_lo(a, b)
                elif what == "add":
                    add_down(a % 4, 2 * b + 2, a + 2)
                elif what.startswith("m_add"):
                    tb, i = int(what[-1]), m_add_index(what, a)
                    if i == 0:
                        dve.wait_ge(g_mlp_landed, 16)
                        dve.wait_ge(acc_added, 4 * FF_STRIPS)
                    if tb == 0:
                        dve.wait_ge(m_block0_done, i + 1)
                    else:
                        dve.wait_ge(half_used, 2 * b + 2)
                    m = acc[:, tb, a * W:(a + 1) * W]
                    nc.vector.tensor_tensor(m, m, ps[:, 4 + 2 * (a % 2) + tb], ALU.add).then_inc(last_added, 1)
                    if a == 2:
                        if tb == 1:
                            finish(0, 0)
                        dve.wait_ge(m_squared, 3 + i)
                        nc.vector.reduce_sum(ss_row[:, tb:tb + 1], ss_strip[:, tb, 0:3], AX_X
                                             ).then_inc(ss_m_ready, 1)
                        nc.vector.tensor_tensor(m, m, g_post_mlp[:, 2 * W:3 * W], ALU.mult).then_inc(m_gained, 1)
                        if tb == 1:
                            finish(0, 1)
                    else:
                        dve.wait_ge(last_added, i + 1)
                        nc.vector.tensor_tensor(gained[:, tb], m, g_post_mlp[:, 3 * W:], ALU.mult
                                                ).then_inc(last_gained, 1)
                        if tb == 1:
                            finish(0, 2)
                            for q in range(DVE_PARTS):
                                finish(1, q)

            for what, a, b in steps:
                step(what, a, b)
            with dve.Fori(LOOP.start, LOOP.stop) as j:
                base = (j - LOOP.start) * 16 + 2 * NQ
                for i in range(16):
                    if i >= 8 and i % 2:
                        add_down((i - 9) // 2, base + (i + 1), (j - 1) * 4 + ((i - 9) // 2 + 2))
                    split_lo(i % AHEAD, (i + AHEAD) // 2 % RAW, (i % 2) * 2 * W, 2 * W,
                             base + (i + AHEAD + 1))
                hidden_lo(j)
            for what, a, b in tail:
                step(what, a, b)

        @block.gpsimd
        def _(pool):
            def own(ins):
                own.count += 1
                ins.then_inc(pool_own, 1)
                pool.wait_ge(pool_own, own.count)
            own.count = 0

            def rstd(dst, ss, parts, ready, norm):
                for cols, n in parts:
                    ins = nc.gpsimd.tensor_scalar(mean_sq[:, norm, cols], ss[:, cols], 1.0 / n, EPS, ALU.mult, ALU.add)
                own(ins)
                width = parts[-1][0].stop
                nc.gpsimd.tensor_tensor(dst[:, 0:width], mean_sq[:, norm, 0:width], neg_half[:, 0:width],
                                        ALU.pow).then_inc(ready, 1)

            def mean_partial(tb, norm):
                own(nc.gpsimd.tensor_scalar(mean_sq[:, norm + tb, 0:1], ss_row[:, tb:tb + 1], 1.0 / D, EPS,
                                            ALU.mult, ALU.add))

            def rstd_last(dst, tb, ready, norm):
                own(nc.gpsimd.tensor_scalar(mean_sq[:, norm + tb, 1:2], ss_strip[:, tb, 3:4], 1.0 / D,
                                            mean_sq[:, norm + tb, 0:1], ALU.mult, ALU.add))
                nc.gpsimd.tensor_tensor(dst[:, tb:tb + 1], mean_sq[:, norm + tb, 1:2], neg_half[:, 0:1], ALU.pow
                                        ).then_inc(ready, 1)

            def scale_y(tb, q):
                pool.wait_ge(y_out, 6 if q < 3 else 8)
                cols = slice(q * W, (q + 1) * W)
                nc.gpsimd.tensor_scalar(acc[:, tb, cols], acc[:, tb, cols], rstd_row[:, tb:tb + 1], None,
                                        ALU.mult).then_inc(y_scaled, 1)

            def rotate(src, cos, sin, dsts, ready):
                n = src.shape[1]
                nc.gpsimd.tensor_tensor(rope_c[:, 0:n], src, cos, ALU.mult)
                own(nc.gpsimd.tensor_tensor(rope_s[:, 0:n], src, sin, ALU.mult))
                lo, hi = slice(0, ROPE // 2), slice(ROPE // 2, ROPE)
                for dst in dsts:
                    nc.gpsimd.tensor_tensor(dst[:, :, lo], rope_c[:, 0:n, lo], rope_s[:, 0:n, hi], ALU.add
                                            ).then_inc(ready, 1)
                    nc.gpsimd.tensor_tensor(dst[:, :, hi], rope_c[:, 0:n, hi], rope_s[:, 0:n, lo], ALU.add
                                            ).then_inc(ready, 1)

            def square(j):
                pool.wait_ge(relu_ready, j + 1)
                a = a_sb.rearrange("p b n -> p (b n)")
                nc.gpsimd.tensor_tensor(a, a, a, ALU.mult).then_inc(a_ready, 1)

            nc.gpsimd.memset(eps_col[:], EPS)
            nc.gpsimd.memset(ones[:], 1.0).then_inc(ones_ready, 1)
            own(nc.gpsimd.memset(neg_half[:], -0.5))

            def step(what, a, b):
                if what == "x_stats":
                    pool.wait_ge(ss_x_ready, 2)
                    rstd(rstd_x, ss_x, [(slice(0, 2), D)], rstd_x_ready, 0)
                elif what == "lat_norm":
                    pool.wait_ge(ss_lat_ready, 4)
                    rstd(rstd_lat, ss_lat, [(slice(0, 2), Q_RANK), (slice(2, 4), KV_RANK)], rstd_lat_ready, 1)
                    pool.wait_ge(tables_landed, 32)
                    pool.wait_ge(strip_out_act, 3)
                    rotate(lat[:, :, Q_RANK + KV_RANK:LAT], cos_t[:, :, 0:ROPE], sin_t[:, :, 0:ROPE],
                           [kr_rot[:, :, 0], kr_rot[:, :, 1]], kr_ready)
                elif what == "q_out":
                    pool.wait_ge(q_ready, a + 1)
                    if a:
                        pool.wait_ge(qrT_filled, a)
                    for tb in range(TB):
                        if a or tb:
                            pool.wait_ge(q_rope_ready, 4 * a + 2 * tb)
                        else:
                            pool.wait_ge(kr_ready, 4)
                        rotate(q_sb[:, tb].rearrange("p (h n) -> p h n", h=2)[:, :, NOPE:],
                               cos_t[:, tb].rearrange("p (h n) -> p h n", h=2),
                               sin_t[:, tb].rearrange("p (h n) -> p h n", h=2), [qr_rot[:, tb]], q_rope_ready)
                elif what == "pv":
                    pool.wait_ge(o_ready, a + 1)
                    if a:
                        pool.wait_ge(ss_o_ready, a)
                    nc.gpsimd.tensor_tensor(o_sq.rearrange("p h b n -> p (h b n)"),
                                            o_sb.rearrange("p h b n -> p (h b n)"),
                                            o_sb.rearrange("p h b n -> p (h b n)"), ALU.mult
                                            ).then_inc(o_sq_ready, 1)
                elif what == "o_squares":
                    pool.wait_ge(ss_o_ready, a + 1)
                    if a:
                        pool.wait_ge(rstd_o_ready, a)
                    rstd(rstd_o, ss_o, [(slice(0, 4), V_DIM)], rstd_o_ready, 2)
                elif what == "y_partial":
                    pool.wait_ge(ss_y_ready, 1)
                    for tb in range(TB):
                        mean_partial(tb, 3)
                elif what == "y_block":
                    pool.wait_ge(y_squared, 7 + a)
                    rstd_last(rstd_row, a, rstd_y_ready, 3)
                    if a == 0:
                        pool.wait_ge(rstd_y_ready, 1)
                        scale_y(0, 2)
                elif what == "x2_stats":
                    pool.wait_ge(ss_x2_ready, 2)
                    rstd(rstd_x2, ss_x, [(slice(0, 2), D)], rstd_x2_ready, 5)
                    for tb in range(TB):
                        nc.gpsimd.memset(acc[:, tb], 0.0).then_inc(acc_added, 1)
                elif what == "x2" and a >= X2_DVE:
                    if a == X2_DVE:
                        pool.wait_ge(rstd_y_ready, 2)
                        scale_y(1, 2)
                    elif a == X2_DVE + 2:
                        scale_y(0, 3)
                        scale_y(1, 3)
                    pool.wait_ge(y_scaled, 2 if a < X2_DVE + 2 else 4)
                    pool.wait_ge(x_res_landed, 16)
                    cols = slice(a * SEQ, (a + 1) * SEQ)
                    nc.gpsimd.tensor_tensor(x_res[:, :, cols], x_res[:, :, cols], acc[:, :, cols], ALU.add
                                            ).then_inc(x2_pool_ready, 1)
                elif what == "relu":
                    square(a)
                elif what == "m_square":
                    pool.wait_ge(m_squared, a + 1)
                    pool.wait_ge(g_mlp_landed, 16)
                    cols = slice(a * W, (a + 1) * W)
                    for tb in range(TB):
                        nc.gpsimd.tensor_tensor(acc[:, tb, cols], acc[:, tb, cols], g_post_mlp[:, cols], ALU.mult
                                                ).then_inc(m_gained_pool, 1)
                elif what.startswith("m_add"):
                    tb, i = int(what[-1]), m_add_index(what, a)
                    if a == 2:
                        pool.wait_ge(ss_m_ready, tb + 1)
                        mean_partial(tb, 6)
                    else:
                        pool.wait_ge(m_squared, 3 + i)
                        rstd_last(rstd_m, tb, rstd_m_ready, 6)
                        pool.wait_ge(scaled_ready, tb + 1)
                        nc.gpsimd.tensor_tensor(x_res[:, tb, 3 * W:], x_res[:, tb, 3 * W:], a_sb[:, tb], ALU.add
                                                ).then_inc(result_pool, 1)

            for what, a, b in steps:
                step(what, a, b)
            with pool.Fori(LOOP.start, LOOP.stop) as j:
                square(j)
            for what, a, b in tail:
                step(what, a, b)


_INS = ["x", "pre_mix_g", "w_in", "conv_w", "q_norm_g", "w_uq", "kv_norm_g", "w_ukv", "conv_out_g",
        "attn_out_g", "w_o", "post_mix_g", "pre_mlp_g", "w_up", "w_down", "post_mlp_g"]
ROPE_THETA = 10000.0


def rope_tables():
    import numpy as np

    inv_freq = np.power(np.float32(ROPE_THETA), -np.arange(0, ROPE, 2, dtype=np.float32) / np.float32(ROPE))
    ang = np.arange(SEQ, dtype=np.float32)[:, None] * inv_freq.astype(np.float32)[None, :]
    cos, sin = np.cos(ang).astype(np.float32), np.sin(ang).astype(np.float32)
    tables = [np.concatenate([cos, cos, cos, cos], 1), np.concatenate([sin, -sin, sin, -sin], 1)]
    return [np.ascontiguousarray(a.reshape(TB, P, 2 * ROPE).transpose(1, 0, 2)) for a in tables]


def gain_table(arrays):
    import numpy as np

    names = ["pre_mix_g", "pre_mlp_g", "q_norm_g", "kv_norm_g", "conv_out_g", "attn_out_g", "conv_w"]
    return np.ascontiguousarray(np.concatenate([arrays[n].reshape(-1, P) for n in names]).T)


def kernel(**inputs):
    import numpy as np
    import concourse.bacc as bacc
    from concourse.bass_utils import run_bass_kernel_spmd

    nc = bacc.Bacc("TRN2", target_bir_lowering=False, num_devices=1)
    arrays = {name: np.ascontiguousarray(inputs[name]) for name in _INS}
    arrays["cos"], arrays["sin"] = rope_tables()
    arrays["ident"] = np.eye(P, dtype=np.float32)
    arrays["gains"] = gain_table(arrays)
    assert arrays["gains"].shape == (P, G_ROWS)
    arrays = {f"in_{name}": a for name, a in arrays.items()}
    t = {name[3:]: nc.dram_tensor(name, a.shape, mybir.dt.from_np(a.dtype), kind="ExternalInput").ap()
         for name, a in arrays.items()}
    out = nc.dram_tensor("out_dram", (1, SEQ, D), F32, kind="ExternalOutput").ap()
    hybrid_block(nc, t, out)
    result = run_bass_kernel_spmd(nc, [arrays], core_ids=[0])
    return result.results[0]["out_dram"]
```
